# Optimizing a Trainium2 kernel written in Bass

```python
import math
import jax, jax.numpy as jnp
from jax import lax
import numpy as np

D_MODEL = 1024
BATCH = 1
SEQ = 256
DEPTH = 1

PLE_DIM = 256
RMS_EPS = 1e-6
A_HEAD_DIM = 64
A_HEADS = D_MODEL // 128
A_WIDTH = A_HEADS * A_HEAD_DIM
MOBA_BLOCK = 256
MOBA_TOPK = 3
Q_CHUNK = 16
REL_BUCKETS = 32
REL_MAX_EXACT = REL_BUCKETS // 2
REL_MAX_DIST = 128
B_HEAD_DIM = 64
B_HEADS = D_MODEL // 128
B_WIDTH = B_HEADS * B_HEAD_DIM
DECAY_RANK = 64
ICLR_RANK = 64
GN_EPS = 64e-5
A_COLS = 4 * A_WIDTH
RW_COLS = 4 * B_WIDTH + DECAY_RANK + ICLR_RANK
IN_COLS = A_COLS + RW_COLS + 2 * D_MODEL


def _rms_norm(x, g):
    xf = x.astype(jnp.float32)
    y = xf * lax.rsqrt(jnp.mean(xf * xf, axis=-1, keepdims=True) + RMS_EPS)
    return y * g.astype(jnp.float32)

def _t5_bucket(dist):
    n = jnp.maximum(dist, 0)
    nf = jnp.maximum(n, 1).astype(jnp.float32)
    large = REL_MAX_EXACT + (jnp.log(nf / REL_MAX_EXACT) / math.log(REL_MAX_DIST / REL_MAX_EXACT)
                             * (REL_BUCKETS - REL_MAX_EXACT)).astype(jnp.int32)
    large = jnp.minimum(large, REL_BUCKETS - 1)
    return jnp.where(n < REL_MAX_EXACT, n, large)

def _moba_attention(q, k, v, rel_bias):
    bsz, seq, nh, hd = q.shape
    n_blk = -(-seq // MOBA_BLOCK)
    pad = n_blk * MOBA_BLOCK - seq
    topk = min(MOBA_TOPK, n_blk)
    qh = jnp.swapaxes(q, 1, 2).astype(jnp.float32) * (hd ** -0.5)
    kh = jnp.pad(jnp.swapaxes(k, 1, 2).astype(jnp.float32), ((0, 0), (0, 0), (0, pad), (0, 0)))
    vh = jnp.pad(jnp.swapaxes(v, 1, 2).astype(jnp.float32), ((0, 0), (0, 0), (0, pad), (0, 0)))
    k_blk = kh.reshape(bsz, nh, n_blk, MOBA_BLOCK, hd)
    v_blk = vh.reshape(bsz, nh, n_blk, MOBA_BLOCK, hd)
    k_mean = jnp.mean(k_blk, axis=3)
    gate = jnp.einsum('bhsd,bhnd->bhsn', qh, k_mean)
    q_blk = jnp.arange(seq) // MOBA_BLOCK
    past = jnp.arange(n_blk)[None, :] < q_blk[:, None]
    gate = jnp.where(past[None, None], gate, -jnp.inf)
    _, sel = lax.top_k(gate, topk)
    bias_h = rel_bias.T.astype(jnp.float32)
    b_idx = jnp.arange(bsz)[:, None, None, None]
    h_idx = jnp.arange(nh)[None, :, None, None]
    offs = jnp.arange(MOBA_BLOCK)

    def chunk(c):
        t0 = c * Q_CHUNK
        pos = t0 + jnp.arange(Q_CHUNK)
        qb = t0 // MOBA_BLOCK
        qc = lax.dynamic_slice_in_dim(qh, t0, Q_CHUNK, axis=2)
        sc = lax.dynamic_slice_in_dim(sel, t0, Q_CHUNK, axis=2)
        ks = k_blk[b_idx, h_idx, sc]
        vs = v_blk[b_idx, h_idx, sc]
        key_pos = sc[..., None] * MOBA_BLOCK + offs
        dist = pos[None, None, :, None, None] - key_pos
        l_sel = jnp.einsum('bhqd,bhqkjd->bhqkj', qc, ks) + bias_h[h_idx[..., None], _t5_bucket(dist)]
        valid = (sc < qb)[..., None]
        l_sel = jnp.where(valid, l_sel, -jnp.inf).reshape(bsz, nh, Q_CHUNK, topk * MOBA_BLOCK)
        ko = lax.dynamic_index_in_dim(k_blk, qb, axis=2, keepdims=False)
        vo = lax.dynamic_index_in_dim(v_blk, qb, axis=2, keepdims=False)
        dist_o = pos[:, None] - (qb * MOBA_BLOCK + offs)[None, :]
        l_own = jnp.einsum('bhqd,bhjd->bhqj', qc, ko) + bias_h[:, _t5_bucket(dist_o)][None]
        l_own = jnp.where((dist_o >= 0)[None, None], l_own, -jnp.inf)
        probs = jax.nn.softmax(jnp.concatenate([l_sel, l_own], axis=-1), axis=-1)
        p_sel = probs[..., :topk * MOBA_BLOCK].reshape(bsz, nh, Q_CHUNK, topk, MOBA_BLOCK)
        p_own = probs[..., topk * MOBA_BLOCK:]
        return (jnp.einsum('bhqkj,bhqkjd->bhqd', p_sel, vs)
                + jnp.einsum('bhqj,bhjd->bhqd', p_own, vo))

    outs = lax.map(chunk, jnp.arange(seq // Q_CHUNK))
    return outs.transpose(1, 0, 3, 2, 4).reshape(bsz, seq, nh * hd)

def _rwkv7_time_mix(cols, mu, w0, w_up, a0, a_up, k_k, k_a, r_k, ln_w, ln_b):
    bsz, seq, _ = cols.shape
    cols = cols.astype(jnp.float32)
    prev = jnp.pad(cols, ((0, 0), (1, 0), (0, 0)))[:, :-1]
    cols = cols + (prev - cols) * mu.astype(jnp.float32)
    o = np.cumsum([0, B_WIDTH, B_WIDTH, B_WIDTH, B_WIDTH, DECAY_RANK])
    r, k, v, z = (cols[..., o[j]:o[j + 1]] for j in range(4))
    wd = cols[..., o[4]:o[5]]
    ad = cols[..., o[5]:]
    w_log = -jax.nn.softplus(-(w0 + jnp.tanh(wd) @ w_up)) - 0.5
    decay = jnp.exp(-jnp.exp(w_log))
    a = jax.nn.sigmoid(a0 + ad @ a_up)
    heads = lambda t: t.reshape(bsz, seq, B_HEADS, B_HEAD_DIM)
    kk = heads(k * k_k)
    kk = kk / jnp.maximum(jnp.linalg.norm(kk, axis=-1, keepdims=True), 1e-12)
    k = k * (1.0 + (a - 1.0) * k_a)
    rh, kh, vh, ah = heads(r), heads(k), heads(v), heads(a)
    xs = tuple(jnp.moveaxis(t, 1, 0) for t in (rh, heads(decay), kh, vh, -kk, kk * ah))

    def step(state, inp):
        r_t, w_t, k_t, v_t, a_t, b_t = inp
        sa = jnp.einsum('bhvk,bhk->bhv', state, a_t)
        state = (state * w_t[:, :, None, :] + sa[..., None] * b_t[:, :, None, :]
                 + v_t[..., None] * k_t[:, :, None, :])
        return state, jnp.einsum('bhvk,bhk->bhv', state, r_t)

    s0 = jnp.zeros((bsz, B_HEADS, B_HEAD_DIM, B_HEAD_DIM), jnp.float32)
    _, y = lax.scan(step, s0, xs)
    y = jnp.moveaxis(y, 0, 1)
    mean = jnp.mean(y, axis=-1, keepdims=True)
    var = jnp.mean(jnp.square(y - mean), axis=-1, keepdims=True)
    y = ((y - mean) * lax.rsqrt(var + GN_EPS)).reshape(bsz, seq, B_WIDTH) * ln_w + ln_b
    bonus = jnp.sum(rh * kh * r_k, axis=-1, keepdims=True) * vh
    y = y + bonus.reshape(bsz, seq, B_WIDTH)
    return y, z

def first_inputs(seed: int = 0) -> dict:
    key = jax.random.key(seed)
    ks = jax.random.split(key, 22)
    n = lambda k, s, sc: jax.random.normal(k, s, jnp.float32) * sc
    L = DEPTH
    return {
        "x": n(ks[0], (BATCH, SEQ, D_MODEL), 1.0),
        "p": n(ks[1], (DEPTH, BATCH, SEQ, PLE_DIM), 1.0),
        "g_pre": 1.0 + n(ks[2], (L, D_MODEL), 0.05),
        "w_in": n(ks[3], (L, D_MODEL, IN_COLS), D_MODEL ** -0.5),
        "rel_bias": n(ks[4], (REL_BUCKETS, A_HEADS), 0.5),
        "mu_shift": jax.random.uniform(ks[5], (L, RW_COLS), jnp.float32, 0.0, 1.0),
        "w0": jax.random.uniform(ks[6], (L, B_WIDTH), jnp.float32, -4.0, 1.0),
        "w_up": n(ks[7], (L, DECAY_RANK, B_WIDTH), 0.5 * DECAY_RANK ** -0.5),
        "a0": n(ks[8], (L, B_WIDTH), 0.5),
        "a_up": n(ks[9], (L, ICLR_RANK, B_WIDTH), 0.5 * ICLR_RANK ** -0.5),
        "k_k": 0.85 + n(ks[10], (L, B_WIDTH), 0.05),
        "k_a": 1.0 + n(ks[11], (L, B_WIDTH), 0.05),
        "r_k": n(ks[12], (L, B_HEADS, B_HEAD_DIM), 0.1),
        "ln_x_w": 1.0 + n(ks[13], (L, B_WIDTH), 0.05),
        "ln_x_b": n(ks[14], (L, B_WIDTH), 0.02),
        "p_a": n(ks[15], (L, A_WIDTH, D_MODEL), A_WIDTH ** -0.5),
        "p_b": n(ks[16], (L, B_WIDTH, D_MODEL), B_WIDTH ** -0.5),
        "w_out": n(ks[17], (L, D_MODEL, D_MODEL), D_MODEL ** -0.5),
        "g_post": 1.0 + n(ks[18], (L, D_MODEL), 0.05),
        "w_ple_up": n(ks[19], (L, PLE_DIM, D_MODEL), PLE_DIM ** -0.5),
        "w_ple_gate": n(ks[20], (L, D_MODEL, D_MODEL), D_MODEL ** -0.5),
    }

def first_block(x, p, g_pre, w_in, rel_bias, mu_shift, w0, w_up, a0, a_up, k_k, k_a, r_k,
              ln_x_w, ln_x_b, p_a, p_b, w_out, g_post, w_ple_up, w_ple_gate):
    bsz, seq, _ = x.shape
    h = x.astype(jnp.float32)
    for i in range(DEPTH):
        u = _rms_norm(h, g_pre[i]).astype(w_in.dtype)
        cols = u @ w_in[i]
        a_cols = cols[..., :A_COLS]
        b_cols = cols[..., A_COLS:A_COLS + RW_COLS]
        gate_a = cols[..., A_COLS + RW_COLS:A_COLS + RW_COLS + D_MODEL].astype(jnp.float32)
        gate_b = cols[..., A_COLS + RW_COLS + D_MODEL:].astype(jnp.float32)
        qa, ka, va, za = (a_cols[..., j * A_WIDTH:(j + 1) * A_WIDTH].reshape(bsz, seq, A_HEADS, A_HEAD_DIM)
                          for j in range(4))
        y_a = _moba_attention(qa, ka, va, rel_bias) * jax.nn.silu(za.reshape(bsz, seq, A_WIDTH).astype(jnp.float32))
        y_b, z_b = _rwkv7_time_mix(b_cols, mu_shift[i], w0[i], w_up[i], a0[i], a_up[i], k_k[i], k_a[i],
                                   r_k[i], ln_x_w[i], ln_x_b[i])
        y_b = y_b * jax.nn.silu(z_b)
        merged = (jax.nn.sigmoid(gate_a) * (y_a.astype(p_a.dtype) @ p_a[i])
                  + jax.nn.sigmoid(gate_b) * (y_b.astype(p_b.dtype) @ p_b[i]))
        y = merged.astype(w_out.dtype) @ w_out[i]
        h = h + _rms_norm(y, g_post[i])
        e = p[i] @ w_ple_up[i]
        h = h + jax.nn.sigmoid((h.astype(w_ple_gate.dtype) @ w_ple_gate[i]).astype(jnp.float32)) * e
    return h.astype(x.dtype)


DEPTH_2 = 2

MLA_HEADS = 4
QK_NOPE = 128
QK_ROPE = 64
V_HEAD = 128
Q_RANK = 384
KV_RANK = 256
ROPE_THETA = 10000.0
Q_BLOCK = 128
HG_HEADS = 4
HG_KEY = 128
HG_VAL = 128
HG_CHUNK = 64
MLA_WIDTH = MLA_HEADS * V_HEAD
HG_WIDTH = HG_HEADS * HG_VAL
HG_FDIM = HG_HEADS * HG_KEY
MIX_WIDTH = MLA_WIDTH + HG_WIDTH
IN_COLS_2 = Q_RANK + KV_RANK + QK_ROPE + 2 * HG_FDIM + 2 * HG_WIDTH
DENSE_FF = 2816
N_EXPERTS = 8
TOP_K = 2
EXPERT_FF = 3584
N_DENSE = (DEPTH_2 + 1) // 2
N_MOE = DEPTH_2 // 2
EPS = 1e-6
F_FLOOR = 1e-30


F32 = jnp.float32
NEG_BIG = float(np.finfo(np.float32).min)

def _rmsnorm(x, gain):
    xf = x.astype(F32)
    y = xf * lax.rsqrt(jnp.mean(xf * xf, axis=-1, keepdims=True) + EPS)
    return (y * gain.astype(F32)).astype(x.dtype)

def _rope_tables(positions):
    inv = ROPE_THETA ** (-jnp.arange(0, QK_ROPE, 2, dtype=F32) / QK_ROPE)
    ang = positions.astype(F32)[..., None] * inv
    return jnp.cos(ang), jnp.sin(ang)

def _apply_rope(x, cos, sin):
    x1, x2 = jnp.split(x, 2, axis=-1)
    cos = cos.astype(x.dtype)
    sin = sin.astype(x.dtype)
    return jnp.concatenate([x1 * cos - x2 * sin, x1 * sin + x2 * cos], axis=-1)

def _mla(c_q, c_kv, k_pe, positions, q_a_norm, w_q_b, kv_a_norm, w_kv_b):
    B, S, _ = c_q.shape
    q = (_rmsnorm(c_q, q_a_norm) @ w_q_b).reshape(B, S, MLA_HEADS, QK_NOPE + QK_ROPE)
    q_nope, q_pe = q[..., :QK_NOPE], q[..., QK_NOPE:]
    cos, sin = _rope_tables(positions)
    q_pe = _apply_rope(q_pe, cos[:, :, None, :], sin[:, :, None, :])
    k_pe = _apply_rope(k_pe, cos, sin)
    kv = (_rmsnorm(c_kv, kv_a_norm) @ w_kv_b).reshape(B, S, MLA_HEADS, QK_NOPE + V_HEAD)
    k_nope, v = kv[..., :QK_NOPE], kv[..., QK_NOPE:]
    scale = (QK_NOPE + QK_ROPE) ** -0.5
    nb = S // Q_BLOCK
    qn_blk = (q_nope * scale).reshape(B, nb, Q_BLOCK, MLA_HEADS, QK_NOPE).transpose(1, 0, 2, 3, 4)
    qp_blk = (q_pe * scale).reshape(B, nb, Q_BLOCK, MLA_HEADS, QK_ROPE).transpose(1, 0, 2, 3, 4)
    starts = jnp.arange(nb, dtype=jnp.int32) * Q_BLOCK
    key_idx = jnp.arange(S, dtype=jnp.int32)

    def block(args):
        qn, qp, start = args
        s = jnp.einsum('bqhd,bkhd->bhqk', qn, k_nope, preferred_element_type=F32)
        s = s + jnp.einsum('bqhr,bkr->bhqk', qp, k_pe, preferred_element_type=F32)
        q_idx = start + jnp.arange(Q_BLOCK, dtype=jnp.int32)
        s = jnp.where(key_idx[None, :] <= q_idx[:, None], s, NEG_BIG)
        p = jax.nn.softmax(s, axis=-1).astype(v.dtype)
        return jnp.einsum('bhqk,bkhd->bqhd', p, v)

    o = lax.map(block, (qn_blk, qp_blk, starts))
    return o.transpose(1, 0, 2, 3, 4).reshape(B, S, MLA_WIDTH)

def _hgrn2(q_raw, f_raw, i_in, g_raw, lower_bound, out_norm):
    B, S, _ = q_raw.shape
    nc = S // HG_CHUNK
    q = jax.nn.silu(q_raw.astype(F32))
    z = f_raw.astype(F32)
    lb = lower_bound.astype(F32)
    f = lb + (1.0 - lb) * jax.nn.sigmoid(z)
    log_f = jnp.log(jnp.maximum(f, F_FLOOR))
    k = (1.0 - lb) * jax.nn.sigmoid(-z)

    def to_chunks(t, d):
        return t.reshape(B, nc, HG_CHUNK, HG_HEADS, d).transpose(1, 0, 3, 2, 4)

    qc = to_chunks(q, HG_KEY)
    kc = to_chunks(k, HG_KEY)
    lfc = to_chunks(log_f, HG_KEY)
    vc = to_chunks(i_in.astype(F32), HG_VAL)
    tri = jnp.tril(jnp.ones((HG_CHUNK, HG_CHUNK), dtype=bool))[:, :, None]

    def step(state, inp):
        qb, kb, vb, lfb = inp
        b = jnp.cumsum(lfb, axis=2)
        diff = b[:, :, :, None, :] - b[:, :, None, :, :]
        decay = jnp.where(tri, jnp.exp(jnp.where(tri, diff, 0.0)), 0.0)
        attn = jnp.einsum('bhtd,bhsd,bhtsd->bhts', qb, kb, decay)
        o = jnp.einsum('bhts,bhsv->bhtv', attn, vb) + jnp.einsum('bhtd,bhdv->bhtv', qb * jnp.exp(b), state)
        b_last = b[:, :, -1:, :]
        new_state = jnp.exp(b_last[:, :, 0, :])[..., None] * state + jnp.einsum('bhsd,bhsv->bhdv', kb * jnp.exp(b_last - b), vb)
        return new_state, o

    s0 = jnp.zeros((B, HG_HEADS, HG_KEY, HG_VAL), F32)
    _, o = lax.scan(step, s0, (qc, kc, vc, lfc))
    o = o.transpose(1, 0, 3, 2, 4).reshape(B, S, HG_HEADS, HG_VAL)
    o = _rmsnorm(o, out_norm) * jax.nn.silu(g_raw.astype(F32).reshape(B, S, HG_HEADS, HG_VAL))
    return o.reshape(B, S, HG_WIDTH)

def _swiglu(h, w_gate, w_up, w_down):
    return (jax.nn.silu(h @ w_gate) * (h @ w_up)) @ w_down

def _moe(h, w_router, w_gate, w_up, w_down):
    B, S, D = h.shape
    T = B * S
    xf = h.reshape(T, D)
    logits = jnp.einsum('td,de->te', xf, w_router, preferred_element_type=F32)
    top_logits, top_idx = lax.top_k(logits, TOP_K)
    gates = jax.nn.softmax(top_logits, axis=-1)
    flat_e = top_idx.reshape(-1)
    flat_tok = jnp.repeat(jnp.arange(T, dtype=jnp.int32), TOP_K)
    order = jnp.argsort(flat_e)
    tok_sorted = flat_tok[order]
    xs = xf[tok_sorted]
    group_sizes = jnp.bincount(flat_e, length=N_EXPERTS).astype(jnp.int32)
    hid = jax.nn.silu(lax.ragged_dot(xs, w_gate, group_sizes)) * lax.ragged_dot(xs, w_up, group_sizes)
    ys = lax.ragged_dot(hid, w_down, group_sizes)
    ys = ys * gates.reshape(-1)[order][:, None].astype(ys.dtype)
    out = jnp.zeros_like(xf).at[tok_sorted].add(ys)
    return out.reshape(B, S, D)

def _normal(key, shape, fan_in):
    return jax.random.normal(key, shape, F32) * (fan_in ** -0.5)

def _gain(key, shape):
    return 1.0 + 0.02 * jax.random.normal(key, shape, F32)

def second_inputs(seed: int = 0) -> dict:
    key = jax.random.key(seed)
    ks = jax.random.split(key, 24)
    x = jax.random.normal(ks[0], (BATCH, SEQ, D_MODEL), F32)
    offset = jax.random.randint(ks[1], (BATCH, 1), 0, 4096, dtype=jnp.int32)
    positions = offset + jnp.arange(SEQ, dtype=jnp.int32)[None, :]
    return {
        "x": x,
        "positions": positions,
        "mix_norm": _gain(ks[2], (DEPTH_2, D_MODEL)),
        "w_in": _normal(ks[3], (DEPTH_2, D_MODEL, IN_COLS_2), D_MODEL),
        "q_a_norm": _gain(ks[4], (DEPTH_2, Q_RANK)),
        "w_q_b": _normal(ks[5], (DEPTH_2, Q_RANK, MLA_HEADS * (QK_NOPE + QK_ROPE)), Q_RANK),
        "kv_a_norm": _gain(ks[6], (DEPTH_2, KV_RANK)),
        "w_kv_b": _normal(ks[7], (DEPTH_2, KV_RANK, MLA_HEADS * (QK_NOPE + V_HEAD)), KV_RANK),
        "hg_lower_bounds": 0.5 * jax.random.normal(ks[8], (DEPTH_2, HG_FDIM), F32),
        "hg_out_norm": _gain(ks[9], (DEPTH_2, HG_VAL)),
        "w_out": _normal(ks[10], (DEPTH_2, MIX_WIDTH, D_MODEL), MIX_WIDTH),
        "ffn_norm": _gain(ks[11], (DEPTH_2, D_MODEL)),
        "dense_w_gate": _normal(ks[12], (N_DENSE, D_MODEL, DENSE_FF), D_MODEL),
        "dense_w_up": _normal(ks[13], (N_DENSE, D_MODEL, DENSE_FF), D_MODEL),
        "dense_w_down": _normal(ks[14], (N_DENSE, DENSE_FF, D_MODEL), DENSE_FF),
        "moe_router": _normal(ks[15], (N_MOE, D_MODEL, N_EXPERTS), D_MODEL),
        "moe_w_gate": _normal(ks[16], (N_MOE, N_EXPERTS, D_MODEL, EXPERT_FF), D_MODEL),
        "moe_w_up": _normal(ks[17], (N_MOE, N_EXPERTS, D_MODEL, EXPERT_FF), D_MODEL),
        "moe_w_down": _normal(ks[18], (N_MOE, N_EXPERTS, EXPERT_FF, D_MODEL), EXPERT_FF),
        "final_norm": _gain(ks[19], (D_MODEL,)),
    }

def second_block(x, positions, mix_norm, w_in, q_a_norm, w_q_b, kv_a_norm, w_kv_b, hg_lower_bounds, hg_out_norm, w_out, ffn_norm, dense_w_gate, dense_w_up, dense_w_down, moe_router, moe_w_gate, moe_w_up, moe_w_down, final_norm):
    lb_p = jax.nn.softmax(hg_lower_bounds.astype(F32), axis=0)
    lower = jnp.cumsum(lb_p, axis=0) - lb_p[0:1]
    splits = np.cumsum([Q_RANK, KV_RANK, QK_ROPE, HG_FDIM, HG_FDIM, HG_WIDTH]).tolist()
    for l in range(DEPTH_2):
        h = _rmsnorm(x, mix_norm[l])
        proj = h @ w_in[l]
        c_q, c_kv, k_pe, hq, hf, hi, hg = jnp.split(proj, splits, axis=-1)
        a = _mla(c_q, c_kv, k_pe, positions, q_a_norm[l], w_q_b[l], kv_a_norm[l], w_kv_b[l])
        r = _hgrn2(hq, hf, hi, hg, lower[l], hg_out_norm[l]).astype(x.dtype)
        x = x + jnp.concatenate([a, r], axis=-1) @ w_out[l]
        h = _rmsnorm(x, ffn_norm[l])
        if l % 2 == 0:
            j = l // 2
            x = x + _swiglu(h, dense_w_gate[j], dense_w_up[j], dense_w_down[j])
        else:
            j = l // 2
            x = x + _moe(h, moe_router[j], moe_w_gate[j], moe_w_up[j], moe_w_down[j])
    return _rmsnorm(x, final_norm)


def setup_inputs(seed=0):
    out = dict(first_inputs(seed))
    for name, value in second_inputs(seed + 1).items():
        if name != "x":
            out[name + "_2"] = value
    return out


def reference(
    x, p, g_pre, w_in, rel_bias, mu_shift, w0, w_up, a0, a_up, k_k, k_a, r_k, ln_x_w, ln_x_b,
    p_a, p_b, w_out, g_post, w_ple_up, w_ple_gate, positions_2, mix_norm_2, w_in_2, q_a_norm_2,
    w_q_b_2, kv_a_norm_2, w_kv_b_2, hg_lower_bounds_2, hg_out_norm_2, w_out_2, ffn_norm_2,
    dense_w_gate_2, dense_w_up_2, dense_w_down_2, moe_router_2, moe_w_gate_2, moe_w_up_2,
    moe_w_down_2, final_norm_2,
):
    x = first_block(
        x, p, g_pre, w_in, rel_bias, mu_shift, w0, w_up, a0, a_up, k_k, k_a, r_k, ln_x_w,
        ln_x_b, p_a, p_b, w_out, g_post, w_ple_up, w_ple_gate,
    )
    return second_block(
        x, positions_2, mix_norm_2, w_in_2, q_a_norm_2, w_q_b_2, kv_a_norm_2, w_kv_b_2,
        hg_lower_bounds_2, hg_out_norm_2, w_out_2, ffn_norm_2, dense_w_gate_2, dense_w_up_2,
        dense_w_down_2, moe_router_2, moe_w_gate_2, moe_w_up_2, moe_w_down_2, final_norm_2,
    )


_drawn_inputs = setup_inputs


def setup_inputs(seed=0):
    import zlib

    import numpy as np

    out = dict(_drawn_inputs(seed))
    spreads = {}
    factors = {'ln_x_b': 2.746,
     'mix_norm_2': 3.002,
     'q_a_norm_2': 8.0,
     'kv_a_norm_2': 5.475,
     'hg_out_norm_2': 4.654,
     'ffn_norm_2': 8.0,
     'hg_lower_bounds_2': 3.458}
    for name, (base, spread) in spreads.items():
        noise = np.random.default_rng([zlib.crc32(name.encode()), seed]).standard_normal(out[name].shape)
        drawn = base * np.exp(spread * noise) if base else spread * noise
        out[name] = __import__('jax').numpy.asarray(drawn.astype(out[name].dtype))
    for name, factor in factors.items():
        out[name] = (out[name] * factor).astype(out[name].dtype)
    return out
```

```python
import math
from contextlib import ExitStack

import numpy as np

import concourse.bass as bass
from concourse import mybir

F32 = mybir.dt.float32
I32 = mybir.dt.int32
U32 = mybir.dt.uint32
ALU = mybir.AluOpType
ACT = mybir.ActivationFunctionType
AX = mybir.AxisListType

P = 128
SEQ = 256
NT = SEQ // P
DM = 1024
KD = DM // P
BANK = 512
BANKS = 8
SLOT = 4096
SLOTS = 7
NEG = -1.0e30
EPS = 1e-6
AH, AD = 8, 64
AW = AH * AD
BW = 512
RW = 4 * BW + 128
CH = 64
REL_BUCKETS, REL_EXACT, REL_DIST = 32, 16, 128
GN_EPS = 64e-5
PLE = 256
HM, NOPE, ROPE, VD = 4, 128, 64, 128
QR, KVR = 384, 256
IN2 = 2752
HH = 4
FF = 2816
NE, EF = 8, 3584
LEVELS = 7
DECAY = -math.exp(-0.5)
TWO_PI_HI = 6.28125
TWO_PI_MID = float(np.float32(2 * math.pi - 6.28125))
TWO_PI_LO = 2 * math.pi - 6.28125 - TWO_PI_MID
PI_SAFE = 3.1415925
ROUND = 12582912.0


def constant_squares():
    i = np.arange(P)
    row, col = i[:, None], i[None, :]
    same_chunk = (row // CH) == (col // CH)
    sq = {
        "ident": row == col,
        "excl": same_chunk & (row < col),
        "incl": same_chunk & (row <= col),
        "before": row < col,
        "upto": row <= col,
        "after": row > col,
        "ones": row + col >= 0,
        "same": same_chunk,
        "carry": (row == P - 1) & (col == 0),
    }
    for n in range(6):
        size = 1 << n
        pair = (row // (2 * size)) == (col // (2 * size))
        sq[f"low{n}"] = pair & ((row // size) % 2 == 1) & ((col // size) % 2 == 0)
    sq["up0"] = sq["low0"].T
    for n in range(LEVELS):
        half = 1 << n
        pair = (row // (2 * half)) == (col // (2 * half))
        right = (col // half) % 2 == 1
        middle = (col // (2 * half)) * 2 * half + half - 1
        sq[f"decay{n}"] = np.where(right, (row > middle) & (row <= col), (row > col) & (row <= middle))
        sq[f"pick{n}"] = pair & ((row // half) % 2 == 0) & ((col // half) % 2 == 1)
    sq["shift"] = (col == row + 1).astype(np.float32) - (col == row)
    return sq


SQUARES = list(constant_squares())


def square_constants():
    return np.concatenate([m.astype(np.float32) for m in constant_squares().values()], axis=1)


def bucket_constants():
    dist = 255 - np.arange(512)
    n = np.maximum(dist, 0)
    nf = np.maximum(n, 1).astype(np.float32)
    large = REL_EXACT + (np.log(nf / REL_EXACT) / math.log(REL_DIST / REL_EXACT)
                         * (REL_BUCKETS - REL_EXACT)).astype(np.int32)
    bucket = np.where(n < REL_EXACT, n, np.minimum(large, REL_BUCKETS - 1))
    out = np.zeros((REL_BUCKETS + 1, 512), np.float32)
    for i in range(512):
        if dist[i] >= 0:
            out[bucket[i], i] = 1.0
        else:
            out[REL_BUCKETS, i] = NEG
    return out


def causal_constants():
    q = np.arange(P)[:, None, None] + P * np.arange(NT)[None, :, None]
    k = np.arange(SEQ)[None, None, :]
    return np.where(k <= q, 0.0, NEG).astype(np.float32).reshape(P, NT * SEQ)


def rope_constants():
    inv = np.float32(10000.0) ** (-np.arange(0, ROPE, 2, dtype=np.float32) / np.float32(ROPE))
    return inv.astype(np.float32).reshape(1, ROPE // 2)


def chunk_constants():
    t = np.arange(P)
    return (t[:, None] // CH == np.arange(2)[None, :]).astype(np.float32)


class Region:

    def __init__(self, whole, size):
        self.whole, self.size, self.at = whole, size, 0

    def take(self, *shape):
        n = int(np.prod(shape))
        assert self.at + n <= self.size, (self.at, n, self.size)
        view = self.whole[:, self.at:self.at + n]
        self.at += n
        if len(shape) == 2:
            return view.rearrange("p (a b) -> p a b", b=shape[1])
        if len(shape) == 3:
            return view.rearrange("p (a b c) -> p a b c", b=shape[1], c=shape[2])
        return view

    def take_top(self, *shape):
        at, end = self.at, self.size
        self.at = self.size = end - int(np.prod(shape))
        assert self.at >= at
        view, self.size = Region(self.whole[:, self.at:end], end - self.at).take(*shape), self.at
        self.at = at
        return view

    def back(self, mark):
        self.at = mark


class Steps:

    def __init__(self, eng, sem):
        self.eng, self.sem, self.n = eng, sem, 0

    def __call__(self, ins):
        self.n += 1
        ins.then_inc(self.sem, 1)
        self.eng.wait_ge(self.sem, self.n)


class Core:

    def __init__(self, nc, ctx):
        self.nc = nc
        self.ctx = ctx
        self.ring = ctx.enter_context(nc.sbuf_tensor("ring", [P, SLOTS, SLOT], F32))
        room = 24536
        self.main = Region(ctx.enter_context(nc.sbuf_tensor("work", [P, room], F32)), room)
        self.ps = [ctx.enter_context(nc.psum_tensor(f"bank{i}", [P, BANK], F32)) for i in range(BANKS)]
        self.landed = [ctx.enter_context(nc.semaphore(f"weights_landed{i}")) for i in range(SLOTS)]
        self.weights_used = ctx.enter_context(nc.semaphore("weights_used"))
        self.plan = []
        self.loaded = 0
        self.consumed = 0
        self.uses = [0] * SLOTS
        self.last_in_slot = [-SLOTS + i for i in range(SLOTS)]
        self.slots_now = SLOTS

    def add_weights(self, src, tiles, width, slots=SLOTS, slot=None):
        if slot is None:
            slot = min(range(slots), key=lambda i: self.last_in_slot[i])
        chunk = dict(slot=slot, src=src, tiles=tiles, width=width,
                     before=self.last_in_slot[slot], landed=16 * (self.uses[slot] + 1))
        self.uses[slot] += 1
        self.last_in_slot[slot] = len(self.plan)
        self.plan.append(chunk)
        return len(self.plan) - 1

    def view(self, n):
        c = self.plan[n]
        return self.ring[:, c["slot"], 0:c["tiles"] * c["width"]].rearrange("p (a n) -> p a n", n=c["width"])

    def load_weights(self, sp, end, most=SLOTS * 100):
        while self.loaded < len(self.plan):
            c = self.plan[self.loaded]
            if c["slot"] >= self.slots_now or c["before"] >= end or self.loaded >= most:
                return
            if c["before"] >= 0:
                sp.wait_ge(self.weights_used, c["before"] + 1)
            sp.dma_start(self.view(self.loaded), c["src"]).then_inc(self.landed[c["slot"]], 16)
            self.loaded += 1

    def wait_weights(self, pe, n):
        pe.wait_ge(self.landed[self.plan[n]["slot"]], self.plan[n]["landed"])


class Phase:

    def __init__(self, core, *names):
        self.core, self.names = core, names

    def __enter__(self):
        self.stack = ExitStack()
        nc = self.core.nc
        self.sems = [self.stack.enter_context(nc.semaphore(n)) for n in self.names]
        return (self.stack.enter_context(nc.Block()), *self.sems)

    def __exit__(self, *a):
        result = self.stack.__exit__(*a)
        for sem in self.sems:
            self.core.nc.gpsimd.sem_clear(sem)
        return result


def wide(ap, n):
    return ap.unsqueeze(1).broadcast_to([ap.shape[0], n, ap.shape[1]])


def tall(ap, n):
    return ap.unsqueeze(2).broadcast_to([ap.shape[0], ap.shape[1], n])


def spread(src, n):
    return src.rearrange("(a n) -> a n", a=1).broadcast_to([n, src.shape[0]])


def gemm(core, lhsT, groups, evacuate, reader, beside=None):
    nc, ps = core.nc, core.ps
    items = [(g, c, tt) for g, (_, cols) in enumerate(groups) for c in range(len(cols)) for tt in range(NT)]
    end = max(ch for parts, _ in groups for ch, _, _ in parts) + 1

    with Phase(core, "product_ready", "emptied_by_vector", "emptied_by_scalar", "vector_steps",
               "scalar_steps") as (block, product_ready, by_vector, by_scalar, vector_steps, scalar_steps):
        emptied = {"vector": by_vector, "scalar": by_scalar}

        @block.sync
        def _(sp):
            core.load_weights(sp, end)

        @block.tensor
        def _(pe):
            first_item, release = 0, False
            for g, (parts, cols) in enumerate(groups):
                mine = [(first_item + n, it) for n, it in enumerate(items[first_item:first_item + NT * len(cols)])]
                for n_part, (ch, k0, tiles) in enumerate(parts):
                    core.wait_weights(pe, ch)
                    w = core.view(ch)
                    for j, (_, c, tt) in mine:
                        c0, width = cols[c]
                        if n_part == 0 and j >= BANKS:
                            who = reader(items[j - BANKS])
                            pe.wait_ge(emptied[who], sum(reader(it) == who for it in items[:j - BANKS + 1]))
                        for kt in range(tiles):
                            mm = pe.matmul(ps[j % BANKS][:, 0:width], lhsT[:, k0 + kt, tt * P:(tt + 1) * P],
                                           w[:, kt, c0:c0 + width], start=(n_part == 0 and kt == 0),
                                           stop=(n_part == len(parts) - 1 and kt == tiles - 1))
                            if release and kt == 0:
                                mm.then_inc(core.weights_used, 1)
                                release = False
                        if n_part == len(parts) - 1:
                            mm.then_inc(product_ready, 1)
                    release = True
                first_item += len(mine)
            pe.wait_ge(product_ready, len(items))
            pe.nop().then_inc(core.weights_used, 1)

        @block.vector
        def _(dve):
            steps = Steps(dve, vector_steps)
            for j, it in enumerate(items):
                if reader(it) == "vector":
                    dve.wait_ge(product_ready, j + 1)
                    evacuate(nc.vector, steps, it, ps[j % BANKS]).then_inc(by_vector, 1)

        @block.scalar
        def _(act):
            steps = Steps(act, scalar_steps)
            if beside is not None:
                beside(act)
            for j, it in enumerate(items):
                if reader(it) == "scalar":
                    act.wait_ge(product_ready, j + 1)
                    evacuate(nc.scalar, steps, it, ps[j % BANKS]).then_inc(by_scalar, 1)
    core.consumed = end


def turn(core, pairs, rms=None, keep=None):
    nc, ps = core.nc, core.ps
    mark = core.main.at
    ident = core.ident
    if rms and keep is None:
        keep = [core.main.take(NT, src.shape[2]) for src, _, _ in pairs]
    n_stat = NT * len(pairs)
    stat = core.main.take(3, n_stat) if rms else None
    rows = keep if rms else [src for src, _, _ in pairs]
    blocks = [(i, tt, k0, min(4, src.shape[2] // P - k0)) for i, (src, _, _) in enumerate(pairs)
              for tt in range(NT) for k0 in range(0, src.shape[2] // P, 4)]

    with Phase(core, "squares_summed", "mean_ready", "root_ready", "scale_ready", "rows_scaled", "turned",
               "copied_by_vector", "copied_by_scalar") as (
            block, squares_summed, mean_ready, root_ready, scale_ready, rows_scaled, turned, by_vector, by_scalar):
        on_vector = [gain is not None or j % 2 == 0 for j, (i, _, _, _) in enumerate(blocks)
                     for gain in [pairs[i][2]]]

        @block.sync
        def _(sp):
            core.load_weights(sp, core.consumed)

        @block.tensor
        def _(pe):
            for j, (i, tt, k0, n) in enumerate(blocks):
                if rms:
                    pe.wait_ge(rows_scaled, i * NT + tt + 1)
                if j >= BANKS:
                    v = on_vector[j - BANKS]
                    pe.wait_ge(by_vector if v else by_scalar,
                               sum(1 for o in on_vector[:j - BANKS + 1] if o == v))
                for k in range(n):
                    mm = pe.transpose(ps[j % BANKS][:, k * P:(k + 1) * P],
                                      rows[i][:, tt, (k0 + k) * P:(k0 + k + 1) * P], ident)
                mm.then_inc(turned, 1)

        @block.vector
        def _(dve):
            if rms:
                for i, (src, _, _) in enumerate(pairs):
                    d = src.shape[2]
                    for tt in range(NT):
                        c = i * NT + tt
                        last = dve.tensor_tensor_reduce(rows[i][:, tt, :], src[:, tt, :], src[:, tt, :], 1.0 / d,
                                                        0.0, ALU.mult, ALU.add, stat[:, 0, c:c + 1])
                last.then_inc(squares_summed, 1)
                dve.wait_ge(squares_summed, 1)
                dve.tensor_scalar(stat[:, 1, :], stat[:, 0, :], EPS, None, ALU.add).then_inc(mean_ready, 1)
                dve.wait_ge(root_ready, 1)
                dve.reciprocal(stat[:, 2, :], stat[:, 1, :]).then_inc(scale_ready, 1)
                dve.wait_ge(scale_ready, 1)
                for i, (src, _, _) in enumerate(pairs):
                    for tt in range(NT):
                        c = i * NT + tt
                        dve.tensor_scalar(rows[i][:, tt, :], src[:, tt, :], stat[:, 2, c:c + 1], None,
                                          ALU.mult).then_inc(rows_scaled, 1)
            for j, (i, tt, k0, n) in enumerate(blocks):
                if on_vector[j]:
                    _, dst, gain = pairs[i]
                    dve.wait_ge(turned, j + 1)
                    out = dst[:, k0:k0 + n, tt * P:(tt + 1) * P]
                    got = ps[j % BANKS][:, 0:n * P].rearrange("p (k t) -> p k t", t=P)
                    if gain is None:
                        dve.tensor_copy(out, got).then_inc(by_vector, 1)
                    else:
                        dve.tensor_tensor(out, got, tall(gain[:, k0:k0 + n], P), ALU.mult).then_inc(by_vector, 1)

        @block.scalar
        def _(act):
            if rms:
                act.wait_ge(mean_ready, 1)
                nc.scalar.activation(stat[:, 1, :], stat[:, 1, :], ACT.Sqrt).then_inc(root_ready, 1)
            for j, (i, tt, k0, n) in enumerate(blocks):
                if not on_vector[j]:
                    act.wait_ge(turned, j + 1)
                    nc.scalar.copy(pairs[i][1][:, k0:k0 + n, tt * P:(tt + 1) * P],
                                   ps[j % BANKS][:, 0:n * P].rearrange("p (k t) -> p k t", t=P)).then_inc(by_scalar, 1)
    core.main.back(mark)


def attention(core, heads, score_parts, scale, bias_of, v_of, finish, width, bias_in=None):
    nc, ps, ident = core.nc, core.ps, core.ident
    mark = core.main.at
    logits = [core.main.take(NT, SEQ) for _ in range(2)]
    probsT = [core.main.take(3, P) for _ in range(2)]
    neg_max = core.main.take(heads, NT)
    total = core.main.take(heads, NT)
    recip = core.main.take(heads, NT)
    blocks = [(0, 0), (1, 0), (1, 1)]

    with Phase(core, "scores_ready", "logits_ready", "max_ready", "probs_ready", "probs_turned", "probsT_ready",
               "mixed", "recip_ready", "rows_out") as (
            block, scores_ready, logits_ready, max_ready, probs_ready, probs_turned, probsT_ready, mixed,
            recip_ready, rows_out):
        @block.sync
        def _(sp):
            core.load_weights(sp, core.consumed)

        @block.tensor
        def _(pe):
            def scores(h):
                if h >= 2:
                    pe.wait_ge(logits_ready, h - 1)
                for tt in range(NT):
                    parts = score_parts(h, tt)
                    for n, (a, b) in enumerate(parts):
                        mm = pe.matmul(ps[h % 2][:, tt * SEQ:(tt + 1) * SEQ], a, b, start=(n == 0),
                                       stop=(n == len(parts) - 1))
                mm.then_inc(scores_ready, 1)

            scores(0)
            for h in range(heads):
                if h + 1 < heads:
                    scores(h + 1)
                pe.wait_ge(probs_ready, NT * (h + 1))
                if h >= 2:
                    pe.wait_ge(probsT_ready, h - 1)
                for n, (tt, kt) in enumerate(blocks):
                    mm = pe.transpose(ps[2 + h % 2][:, n * P:(n + 1) * P],
                                      logits[h % 2][:, tt, kt * P:(kt + 1) * P], ident)
                mm.then_inc(probs_turned, 1)
                pe.wait_ge(probsT_ready, h + 1)
                if h >= 2:
                    pe.wait_ge(rows_out, h - 1)
                out = ps[4 + h % 2]
                pe.matmul(out[:, 0:width], probsT[h % 2][:, 0, :], v_of(h, 0), start=True, stop=True)
                pe.matmul(out[:, width:2 * width], probsT[h % 2][:, 1, :], v_of(h, 0), start=True, stop=False)
                pe.matmul(out[:, width:2 * width], probsT[h % 2][:, 2, :], v_of(h, 1), start=False,
                          stop=True).then_inc(mixed, 1)

        @block.vector
        def _(dve):
            def soften(h):
                dve.wait_ge(scores_ready, h + 1)
                if h >= 2:
                    dve.wait_ge(probs_turned, h - 1)
                dve.scalar_tensor_tensor(out=logits[h % 2], in0=ps[h % 2][:, :].rearrange("p (t k) -> p t k", t=NT),
                                         scalar=scale, in1=bias_of(h).rearrange("p (t k) -> p t k", t=NT),
                                         op0=ALU.mult, op1=ALU.add).then_inc(logits_ready, 1)
                dve.wait_ge(logits_ready, h + 1)
                dve.tensor_reduce(neg_max[:, h, :], logits[h % 2], AX.X, ALU.max, negate=True).then_inc(max_ready, 1)

            if bias_in is not None:
                dve.wait_ge(*bias_in)
            soften(0)
            for h in range(heads):
                if h + 1 < heads:
                    soften(h + 1)
                dve.wait_ge(probs_ready, NT * (h + 1))
                dve.reciprocal(recip[:, h, :], total[:, h, :]).then_inc(recip_ready, 1)
                dve.wait_ge(probs_turned, h + 1)
                if h >= 2:
                    dve.wait_ge(mixed, h - 1)
                dve.tensor_copy(probsT[h % 2], ps[2 + h % 2][:, 0:3 * P].rearrange("p (n t) -> p n t", t=P))\
                   .then_inc(probsT_ready, 1)
                dve.wait_ge(recip_ready, h + 1)
                dve.wait_ge(mixed, h + 1)
                for tt in range(NT):
                    last = finish(dve, h, tt, ps[4 + h % 2][:, tt * width:(tt + 1) * width], recip[:, h, tt:tt + 1])
                last.then_inc(rows_out, 1)

        @block.scalar
        def _(act):
            for h in range(heads):
                act.wait_ge(max_ready, h + 1)
                for tt in range(NT):
                    nc.scalar.activation(logits[h % 2][:, tt, :], logits[h % 2][:, tt, :], ACT.Exp,
                                         bias=neg_max[:, h, tt:tt + 1], accum_out=total[:, h, tt:tt + 1])\
                       .then_inc(probs_ready, 1)
    core.main.back(mark)


def load_squares(core, sp, sem, *names, to=None):
    for n in names:
        i = SQUARES.index(n)
        sp.dma_start(to[n], core.squares[:, i * P:(i + 1) * P]).then_inc(sem, 16)


def rwkv(core, rw, yb, a):
    nc, ps = core.nc, core.ps
    main, scratch = core.main, core.scratch
    outer = (main.at, scratch.at)
    eC = main.take(2 * 4 * 2)
    bonus = main.take(2 * AH)
    names = ("excl", "incl", "same", "low0", "low1", "low2", "low3", "low4", "low5", "up0")
    masks = main.take(2 * P)
    sq = {n: main.take(P) for n in names[2:]}
    sq["excl"], sq["incl"] = masks[:, 0:P], masks[:, P:2 * P]
    pairs_of = main.take(2)
    inner = (main.at, scratch.at)

    mu = scratch.take(RW)
    moved = [scratch.take(BANK) for _ in range(4)]
    shift, carry = scratch.take(P), scratch.take(P)
    widths = [(c, min(BANK, RW - c)) for c in range(0, RW, BANK)]
    with Phase(core, "constants_in", "matrices_in", "differences", "scaled", "added") as (
            block, constants_in, matrices_in, differences, scaled, added):
        @block.sync
        def _(sp):
            sp.dma_start(mu, spread(a["mu_shift"][0], P)).then_inc(constants_in, 16)
            load_squares(core, sp, matrices_in, "shift", "carry", to=dict(shift=shift, carry=carry))
            load_squares(core, sp, matrices_in, *names, to=sq)
            sp.dma_start(pairs_of, core.chunk_pairs).then_inc(matrices_in, 16)
            core.load_weights(sp, core.consumed)
            sp.wait_ge(matrices_in, 16 * (3 + len(names)))

        @block.tensor
        def _(pe):
            pe.wait_ge(matrices_in, 16 * (3 + len(names)))
            for n, (c0, w) in enumerate(widths):
                if n >= 4:
                    pe.wait_ge(scaled, 2 * (n - 3))
                pe.matmul(ps[2 * n % BANKS][:, 0:w], shift, rw[:, 0, c0:c0 + w], start=True, stop=True)
                pe.matmul(ps[(2 * n + 1) % BANKS][:, 0:w], shift, rw[:, 1, c0:c0 + w], start=True, stop=False)
                pe.matmul(ps[(2 * n + 1) % BANKS][:, 0:w], carry, rw[:, 0, c0:c0 + w], start=False,
                          stop=True).then_inc(differences, 1)

        @block.vector
        def _(dve):
            dve.wait_ge(constants_in, 16)
            for n, (c0, w) in enumerate(widths):
                dve.wait_ge(differences, n + 1)
                for tt in range(NT):
                    j = 2 * n + tt
                    if j >= 4:
                        dve.wait_ge(added, j - 3)
                    dve.tensor_tensor(moved[j % 4][:, 0:w], ps[j % BANKS][:, 0:w], mu[:, c0:c0 + w], ALU.mult)\
                       .then_inc(scaled, 1)

        @block.gpsimd
        def _(pool):
            for n, (c0, w) in enumerate(widths):
                for tt in range(NT):
                    j = 2 * n + tt
                    pool.wait_ge(scaled, j + 1)
                    pool.tensor_tensor(rw[:, tt, c0:c0 + w], rw[:, tt, c0:c0 + w], moved[j % 4][:, 0:w], ALU.add)\
                        .then_inc(added, 1)
    scratch.back(inner[1])

    r, k, v, z = (rw[:, :, i * BW:(i + 1) * BW] for i in range(4))
    rt, kt, bt, at = (scratch.take(NT, BW) for _ in range(4))
    keep = scratch.at
    decay, rate, kk, kp, e_ex = (main.take(NT, BW) for _ in range(5))
    tmp = scratch.take(NT, BW)
    e_in, e_neg = scratch.take(NT, BW), scratch.take(NT, BW)
    params = main.take(5, BW)
    w0, a0, k_k, k_a, r_k = (params[:, i, :] for i in range(5))
    up = scratch.take(BW)
    codesT = main.take(SEQ)
    norm = main.take(3, 2 * BW // CH)
    with Phase(core, "parameters_in", "ups_in", "tanh_ready", "codes_turned", "codesT_ready", "low_rank_ready",
               "shifted_ready", "sigmoid_ready", "decays_summed", "exp_ready", "norm_squared", "norm_ready",
               "vector_steps") as (
            block, parameters_in, ups_in, tanh_ready, codes_turned, codesT_ready, low_rank_ready, shifted_ready,
            sigmoid_ready, decays_summed, exp_ready, norm_squared, norm_ready, vector_steps):
        @block.sync
        def _(sp):
            sp.dma_start(up[0:64, :], a["w_up"][0]).then_inc(ups_in, 16)
            sp.dma_start(up[64:128, :], a["a_up"][0]).then_inc(ups_in, 16)
            for i, src in enumerate((a["w0"][0], a["a0"][0], a["k_k"][0], a["k_a"][0],
                                     a["r_k"][0].rearrange("h d -> (h d)"))):
                sp.dma_start(params[:, i, :], spread(src, P)).then_inc(parameters_in, 16)

        @block.tensor
        def _(pe):
            pe.wait_ge(tanh_ready, NT)
            for tt in range(NT):
                mm = pe.transpose(ps[0][:, tt * P:(tt + 1) * P], rw[:, tt, 4 * BW:RW], core.ident)
            mm.then_inc(codes_turned, 1)
            pe.wait_ge(codesT_ready, 1)
            pe.wait_ge(ups_in, 32)
            for tt in range(NT):
                pe.matmul(ps[1 + tt][:, :], codesT[0:64, tt * P:(tt + 1) * P], up[0:64, :], start=True, stop=True)\
                  .then_inc(low_rank_ready, 1)
            for tt in range(NT):
                pe.matmul(ps[3 + tt][:, :], codesT[64:128, tt * P:(tt + 1) * P], up[64:128, :], start=True,
                          stop=True).then_inc(low_rank_ready, 1)
            pe.wait_ge(sigmoid_ready, 2)
            for tt in range(NT):
                pe.matmul(ps[5 + tt][:, :], sq["incl"], decay[:, tt, :], start=True, stop=True)
            for tt in range(NT):
                pe.matmul(ps[(7 + tt) % BANKS][:, :], sq["excl"], decay[:, tt, :], start=True, stop=True)
            for tt in range(NT):
                for pair in range(4):
                    i = 2 * (4 * tt + pair)
                    mm = pe.matmul(ps[1][:, i:i + 2], decay[:, tt, pair * P:(pair + 1) * P], pairs_of,
                                   start=True, stop=True)
            mm.then_inc(decays_summed, 1)

        @block.scalar
        def _(act):
            for tt in range(NT):
                nc.scalar.activation(rw[:, tt, 4 * BW:4 * BW + 64], rw[:, tt, 4 * BW:4 * BW + 64], ACT.Tanh)\
                  .then_inc(tanh_ready, 1)
            for n in range(4):
                act.wait_ge(shifted_ready, n + 1)
                t = (decay, rate)[n // 2][:, n % 2, :]
                nc.scalar.activation(t, t, ACT.Sigmoid).then_inc(sigmoid_ready, 1)
            act.wait_ge(norm_squared, 1)
            nc.scalar.activation(norm[:, 1, :], norm[:, 0, :], ACT.Sqrt).then_inc(norm_ready, 1)
            act.wait_ge(decays_summed, 1)
            for tt in range(NT):
                nc.scalar.activation(e_in[:, tt, :], ps[5 + tt][:, :], ACT.Exp, scale=DECAY)
                nc.scalar.activation(e_neg[:, tt, :], ps[5 + tt][:, :], ACT.Exp, scale=-DECAY)
                nc.scalar.activation(e_ex[:, tt, :], ps[(7 + tt) % BANKS][:, :], ACT.Exp, scale=DECAY)
            nc.scalar.activation(eC, ps[1][:, 0:16], ACT.Exp, scale=DECAY).then_inc(exp_ready, 1)

        @block.vector
        def _(dve):
            step = Steps(dve, vector_steps)
            dve.wait_ge(codes_turned, 1)
            dve.tensor_copy(codesT, ps[0][:, 0:SEQ]).then_inc(codesT_ready, 1)
            dve.wait_ge(parameters_in, 16 * 5)
            for n, (dst, bias) in enumerate(((decay, w0), (rate, a0))):
                for tt in range(NT):
                    dve.wait_ge(low_rank_ready, 2 * n + tt + 1)
                    dve.tensor_tensor(dst[:, tt, :], ps[1 + 2 * n + tt][:, :], bias, ALU.add).then_inc(shifted_ready, 1)
            step(dve.tensor_tensor(tmp, k, wide(k_k, NT), ALU.mult))
            step(dve.tensor_tensor(kk, tmp, tmp, ALU.mult))
            dve.tensor_reduce(norm[:, 0, :], kk.rearrange("p t (h d) -> p (t h) d", d=64), AX.X, ALU.add)\
               .then_inc(norm_squared, 1)
            step(dve.tensor_tensor(rt, r, wide(r_k, NT), ALU.mult))
            dve.wait_ge(norm_ready, 1)
            step(dve.tensor_scalar(norm[:, 1, :], norm[:, 1, :], 1e-12, None, ALU.max))
            step(dve.reciprocal(norm[:, 2, :], norm[:, 1, :]))
            step(dve.tensor_tensor(kk.rearrange("p t (h d) -> p (t h) d", d=64),
                                   tmp.rearrange("p t (h d) -> p (t h) d", d=64), tall(norm[:, 2, :], 64), ALU.mult))
            dve.wait_ge(sigmoid_ready, 4)
            step(dve.scalar_tensor_tensor(out=kp, in0=rate, scalar=-1.0, in1=wide(k_a, NT), op0=ALU.add, op1=ALU.mult))
            step(dve.scalar_tensor_tensor(out=kp, in0=kp, scalar=1.0, in1=k, op0=ALU.add, op1=ALU.mult))
            step(dve.tensor_tensor(rt, rt, kp, ALU.mult))
            step(dve.tensor_reduce(bonus, rt.rearrange("p t (h d) -> p (t h) d", d=64), AX.X, ALU.add))
            step(dve.tensor_tensor(bt, kk, rate, ALU.mult))
            dve.wait_ge(exp_ready, 1)
            step(dve.tensor_tensor(rt, r, e_in, ALU.mult))
            step(dve.tensor_tensor(kt, kp, e_neg, ALU.mult))
            step(dve.tensor_tensor(bt, bt, e_neg, ALU.mult))
            step(dve.scalar_tensor_tensor(out=at, in0=kk, scalar=-1.0, in1=e_ex, op0=ALU.mult, op1=ALU.mult))
    main.back(inner[0])
    scratch.back(keep)

    y = main.take(NT, BW)
    state = main.take(4, P)
    arT = main.take(4, 2 * P)
    scores = main.take(AH, 4 * P)
    spare = main.at
    bkT = scratch.take(AH, 2 * P)
    xT = main.take(AH, P)
    x = scratch.take(AH, P)
    work = scratch.take(AH, P)
    for tt in range(NT):
        with Phase(core, "zeroed", "turned", "copied_by_vector", "copied_by_scalar", "scored", "masked",
                   "lower_ready", "inverse_ready", "first_product", "first_masked", "update_ready",
                   "vector_steps") as (
                block, zeroed, turned, by_vector, by_scalar, scored, masked, lower_ready, inverse_ready,
                first_product, first_masked, update_ready, vector_steps):
            ar = arT.rearrange("p n (two t) -> p n two t", two=2)
            bk = bkT.rearrange("p (n par) (two t) -> p n par two t", par=2, two=2)

            @block.sync
            def _(sp):
                core.load_weights(sp, core.consumed)

            @block.gpsimd
            def _(pool):
                pool.memset(bk[64:128, :, 0, :, :].rearrange("p n two t -> p n (two t)"), 0.0).then_inc(zeroed, 1)
                pool.memset(bk[0:64, :, 1, :, :].rearrange("p n two t -> p n (two t)"), 0.0).then_inc(zeroed, 1)

            @block.tensor
            def _(pe):
                for n, src in enumerate((at, rt, bt, kt)):
                    for pair in range(4):
                        mm = pe.transpose(ps[n][:, pair * P:(pair + 1) * P], src[:, tt, pair * P:(pair + 1) * P],
                                          core.ident)
                    mm.then_inc(turned, 1)
                pe.wait_ge(zeroed, 2)
                pe.wait_ge(by_vector, 3)
                pe.wait_ge(by_scalar, 3)
                for h in range(AH):
                    bank = ps[4 + h % 4]
                    if h >= 4:
                        pe.wait_ge(masked, h - 3)
                    for n in range(2):
                        mm = pe.matmul(bank[:, 2 * n * P:2 * (n + 1) * P], bkT[:, h, n * P:(n + 1) * P],
                                       arT[:, h // 2, :], start=True, stop=True)
                    mm.then_inc(scored, 1)
                for h in range(AH):
                    mm = pe.matmul(ps[h // 4][:, (h % 4) * P:(h % 4 + 1) * P], arT[:, h // 2, 0:P], bkT[:, h, 0:P],
                                   start=True, stop=True)
                    if h % 4 == 3:
                        mm.then_inc(lower_ready, 1)
                for n in range(1, 6):
                    for g in range(2):
                        pe.wait_ge(inverse_ready, 2 * (n - 1) + g + 1)
                        for h in range(4 * g, 4 * g + 4):
                            mm = pe.matmul(ps[2 + g][:, (h % 4) * P:(h % 4 + 1) * P], scores[:, h, 0:P], x[:, h, :],
                                           start=True, stop=True)
                        mm.then_inc(first_product, 1)
                    for g in range(2):
                        pe.wait_ge(first_masked, 2 * (n - 1) + g + 1)
                        for h in range(4 * g, 4 * g + 4):
                            mm = pe.matmul(ps[4 + g][:, (h % 4) * P:(h % 4 + 1) * P], work[:, h, :], xT[:, h, :],
                                           start=True, stop=True)
                        if n < 5:
                            for h in range(4 * g, 4 * g + 4):
                                mm = pe.matmul(ps[6 + g][:, (h % 4) * P:(h % 4 + 1) * P], xT[:, h, :], work[:, h, :],
                                               start=True, stop=True)
                        mm.then_inc(update_ready, 1)

            @block.scalar
            def _(act):
                act.wait_ge(turned, 2)
                nc.scalar.copy(ar[:, :, 1, :], ps[1][:, :].rearrange("p (n t) -> p n t", t=P)).then_inc(by_scalar, 1)
                act.wait_ge(turned, 4)
                for par in range(2):
                    rows = slice(64 * par, 64 * par + 64)
                    nc.scalar.copy(bk[rows, :, par, 1, :], ps[3][rows, :].rearrange("p (n t) -> p n t", t=P))\
                      .then_inc(by_scalar, 1)

            @block.vector
            def _(dve):
                step = Steps(dve, vector_steps)
                dve.wait_ge(turned, 1)
                dve.tensor_copy(ar[:, :, 0, :], ps[0][:, :].rearrange("p (n t) -> p n t", t=P)).then_inc(by_vector, 1)
                dve.wait_ge(turned, 3)
                for par in range(2):
                    rows = slice(64 * par, 64 * par + 64)
                    dve.tensor_copy(bk[rows, :, par, 0, :], ps[2][rows, :].rearrange("p (n t) -> p n t", t=P))\
                       .then_inc(by_vector, 1)
                for h in range(AH):
                    dve.wait_ge(scored, h + 1)
                    for n in range(2):
                        src = ps[4 + h % 4][:, 2 * n * P:2 * (n + 1) * P]
                        last = dve.tensor_tensor(scores[:, h, 2 * n * P:2 * (n + 1) * P], src, masks, ALU.mult)
                    last.then_inc(masked, 1)
                dve.wait_ge(masked, AH)
                for g in range(2):
                    heads = slice(4 * g, 4 * g + 4)
                    dve.wait_ge(lower_ready, g + 1)
                    step(dve.tensor_tensor(x[:, heads, :], ps[g][:, :].rearrange("p (n t) -> p n t", t=P),
                                           wide(sq["low0"], 4), ALU.mult))
                    step(dve.tensor_tensor(x[:, heads, :], x[:, heads, :], wide(core.ident, 4), ALU.add))
                    step(dve.tensor_tensor(xT[:, heads, :], scores[:, heads, 0:P], wide(sq["up0"], 4), ALU.mult))
                    dve.tensor_tensor(xT[:, heads, :], xT[:, heads, :], wide(core.ident, 4), ALU.add)\
                       .then_inc(inverse_ready, 1)
                for n in range(1, 6):
                    for g in range(2):
                        dve.wait_ge(first_product, 2 * (n - 1) + g + 1)
                        dve.tensor_tensor(work[:, 4 * g:4 * g + 4, :], ps[2 + g][:, :].rearrange("p (n t) -> p n t", t=P),
                                          wide(sq[f"low{n}"], 4), ALU.mult).then_inc(first_masked, 1)
                    for g in range(2):
                        heads = slice(4 * g, 4 * g + 4)
                        dve.wait_ge(update_ready, 2 * (n - 1) + g + 1)
                        if n < 5:
                            dve.tensor_tensor(x[:, heads, :], x[:, heads, :],
                                              ps[6 + g][:, :].rearrange("p (n t) -> p n t", t=P), ALU.add)
                        dve.tensor_tensor(xT[:, heads, :], xT[:, heads, :],
                                          ps[4 + g][:, :].rearrange("p (n t) -> p n t", t=P), ALU.add)\
                           .then_inc(inverse_ready, 1)

        x_mark, work_mark = x, work
        rhs = x_mark[:, 0:4, :].rearrange("p n t -> p (n t)")
        carried = work_mark[:, 0:4, :].rearrange("p n t -> p (n t)")
        u_all = x_mark[:, 4:8, :].rearrange("p n t -> p (n t)")
        u_of = [bkT[:, 2 * c:2 * c + 2, :].rearrange("p n t -> p (n t)") for c in range(2)]
        v_of = [bkT[:, 4 + 2 * c:6 + 2 * c, :].rearrange("p n t -> p (n t)") for c in range(2)]
        fall = work_mark[:, 4:8, :]
        with Phase(core, "zeroed", "values_split", "state_ready", "right_side", "right_copied", "read_state",
                   "solved", "solution_split", "solution_whole", "gained", "parts_ready", "parts_copied",
                   "vector_steps") as (
                block, zeroed, values_split, state_ready, right_side, right_copied, read_state, solved,
                solution_split, solution_whole, gained, parts_ready, parts_copied, vector_steps):
            @block.sync
            def _(sp):
                core.load_weights(sp, core.consumed)

            @block.gpsimd
            def _(pool):
                for c in range(2):
                    other = slice(64 * (1 - c), 64 * (1 - c) + 64)
                    own = slice(64 * c, 64 * c + 64)
                    pool.memset(u_of[c][other, :], 0.0).then_inc(zeroed, 1)
                    pool.memset(v_of[c][other, :], 0.0).then_inc(values_split, 1)
                    pool.tensor_copy(v_of[c][own, :], v[own, tt, :]).then_inc(values_split, 1)

            @block.tensor
            def _(pe):
                for c in range(2):
                    pe.wait_ge(state_ready, c + 1)
                    if c:
                        pe.wait_ge(right_copied, 1)
                    for h in range(AH):
                        pe.matmul(ps[c][:, h * 64:(h + 1) * 64], scores[:, h, 2 * P:3 * P], v[:, tt, h * 64:(h + 1) * 64],
                                  start=(h == 0), stop=False, skip_group_check=True)
                    for pair in range(4):
                        mm = pe.matmul(ps[c][:, pair * P:(pair + 1) * P], arT[:, pair, 0:P], state[:, pair, :],
                                       start=False, stop=(pair == 3), skip_group_check=True)
                    mm.then_inc(right_side, 1)
                    for pair in range(4):
                        mm = pe.matmul(ps[4 + 2 * c][:, pair * P:(pair + 1) * P], arT[:, pair, P:2 * P],
                                       state[:, pair, :], start=True, stop=True)
                    mm.then_inc(read_state, 1)
                    pe.wait_ge(right_copied, c + 1)
                    for h in range(AH):
                        mm = pe.matmul(ps[2][:, h * 64:(h + 1) * 64], xT[:, h, :], rhs[:, h * 64:(h + 1) * 64],
                                       start=True, stop=True)
                    mm.then_inc(solved, 1)
                    pe.wait_ge(values_split, 4)
                    pe.wait_ge(solution_split, c + 1)
                    pe.wait_ge(zeroed, 2)
                    for pair in range(4):
                        cols = slice(pair * P, (pair + 1) * P)
                        pe.matmul(ps[3][:, cols], kt[:, tt, cols], v_of[c][:, cols], start=True, stop=False)
                        mm = pe.matmul(ps[3][:, cols], bt[:, tt, cols], u_of[c][:, cols], start=False, stop=True)
                    mm.then_inc(gained, 1)
                    pe.wait_ge(solution_whole, c + 1)
                for h in range(AH):
                    cols = slice(h * 64, (h + 1) * 64)
                    pe.matmul(ps[5][:, cols], scores[:, h, 3 * P:4 * P], v[:, tt, cols], start=True, stop=False)
                    mm = pe.matmul(ps[5][:, cols], scores[:, h, P:2 * P], u_all[:, cols], start=False, stop=True)
                mm.then_inc(parts_ready, 1)

            @block.scalar
            def _(act):
                for c in range(2):
                    own = slice(64 * c, 64 * c + 64)
                    act.wait_ge(right_side, c + 1)
                    nc.scalar.copy(rhs, ps[c][:, :]).then_inc(right_copied, 1)
                    act.wait_ge(read_state, c + 1)
                    nc.scalar.copy(carried[own, :], ps[4 + 2 * c][own, :]).then_inc(parts_copied, 1)
                    act.wait_ge(solved, c + 1)
                    act.wait_ge(solution_split, c + 1)
                    nc.scalar.copy(u_all[own, :], ps[2][own, :]).then_inc(solution_whole, 1)

            @block.vector
            def _(dve):
                step = Steps(dve, vector_steps)
                if tt == 0:
                    dve.memset(state, 0.0).then_inc(state_ready, 1)
                else:
                    dve.nop().then_inc(state_ready, 1)
                for c in range(2):
                    own = slice(64 * c, 64 * c + 64)
                    dve.wait_ge(solved, c + 1)
                    dve.tensor_copy(u_of[c][own, :], ps[2][own, :]).then_inc(solution_split, 1)
                    i = 8 * tt + c
                    step(dve.tensor_tensor(fall, wide(sq["same"], 4), tall(eC[:, i:i + 7:2], P), ALU.mult))
                    dve.wait_ge(gained, c + 1)
                    dve.wait_ge(read_state, c + 1)
                    step(dve.tensor_tensor(state, state, ps[3][:, :].rearrange("p (n t) -> p n t", t=P), ALU.add))
                    dve.tensor_tensor(state, state, fall, ALU.mult).then_inc(state_ready, 1)
                dve.wait_ge(parts_ready, 1)
                dve.wait_ge(parts_copied, 2)
                step(dve.tensor_tensor(y[:, tt, :], carried, ps[5][:, :], ALU.add))
    main.back(spare)
    scratch.back(keep)

    ln = main.take(2, BW)
    stat = main.take(4, 2 * AH)
    sqr = scratch.take(NT, BW)
    gate = scratch.take(NT, BW)
    extra = scratch.take(NT, BW)
    by_head = lambda t: t.rearrange("p t (h d) -> p (t h) d", d=64)
    with Phase(core, "norms_in", "var_ready", "root_ready", "gate_ready", "bonus_ready", "vector_steps") as (
            block, norms_in, var_ready, root_ready, gate_ready, bonus_ready, vector_steps):
        @block.sync
        def _(sp):
            sp.dma_start(ln[:, 0, :], spread(a["ln_x_w"][0], P)).then_inc(norms_in, 16)
            sp.dma_start(ln[:, 1, :], spread(a["ln_x_b"][0], P)).then_inc(norms_in, 16)
            core.load_weights(sp, core.consumed)

        @block.scalar
        def _(act):
            act.wait_ge(var_ready, 1)
            nc.scalar.activation(stat[:, 2, :], stat[:, 1, :], ACT.Sqrt).then_inc(root_ready, 1)
            nc.scalar.activation(gate, z, ACT.Silu).then_inc(gate_ready, 1)

        @block.gpsimd
        def _(pool):
            pool.tensor_tensor(extra.rearrange("p t (h d) -> p t h d", d=64),
                               v.rearrange("p t (h d) -> p t h d", d=64),
                               bonus.rearrange("p (t h) -> p t h", t=NT).unsqueeze(3).broadcast_to([P, NT, AH, 64]),
                               ALU.mult).then_inc(bonus_ready, 1)

        @block.vector
        def _(dve):
            step = Steps(dve, vector_steps)
            step(dve.tensor_reduce(stat[:, 0, :], by_head(y), AX.X, ALU.add))
            step(dve.tensor_scalar(stat[:, 0, :], stat[:, 0, :], 1.0 / 64, None, ALU.mult))
            step(dve.tensor_tensor(by_head(y), by_head(y), tall(stat[:, 0, :], 64), ALU.subtract))
            step(dve.tensor_tensor(sqr, y, y, ALU.mult))
            step(dve.tensor_reduce(stat[:, 1, :], by_head(sqr), AX.X, ALU.add))
            dve.tensor_scalar(stat[:, 1, :], stat[:, 1, :], 1.0 / 64, GN_EPS, ALU.mult, ALU.add).then_inc(var_ready, 1)
            dve.wait_ge(root_ready, 1)
            step(dve.reciprocal(stat[:, 3, :], stat[:, 2, :]))
            step(dve.tensor_tensor(by_head(y), by_head(y), tall(stat[:, 3, :], 64), ALU.mult))
            dve.wait_ge(norms_in, 32)
            step(dve.tensor_tensor(y, y, wide(ln[:, 0, :], NT), ALU.mult))
            step(dve.tensor_tensor(y, y, wide(ln[:, 1, :], NT), ALU.add))
            dve.wait_ge(bonus_ready, 1)
            step(dve.tensor_tensor(y, y, extra, ALU.add))
            dve.wait_ge(gate_ready, 1)
            step(dve.tensor_tensor(yb, y, gate, ALU.mult))
    main.back(outer[0])
    scratch.back(outer[1])


def begin(core, a, bias, rows, gains, sources):
    nc, ps, h, cos, sin = core.nc, core.ps, core.h, core.cos, core.sin
    mark = core.main.at
    table = core.main.take(AH)
    wide_table = core.main.take(AH, P)
    marking = core.main.take(BANK)
    pos_i = core.main.take(NT).bitcast(I32)
    pos = core.main.take(NT)
    inv = core.main.take(ROPE // 2)
    angle, turns, tmp = (core.main.take(NT, ROPE // 2) for _ in range(3))
    core.lines = line = nc.dram_tensor("bias_lines", (AH, P * BANK + BANK), F32, kind="Internal").ap()
    with Phase(core, "table_in", "marking_in", "last_row", "table_wide", "rows_ready", "rows_copied",
               "positions_in", "rows_in", "reduced", "vector_steps") as (
            block, table_in, marking_in, last_row, table_wide, rows_ready, rows_copied, positions_in, rows_in,
            reduced, vector_steps):
        @block.sync
        def _(sp):
            sp.dma_start(h, a["x"][0].rearrange("(t p) d -> p t d", p=P)).then_inc(rows_in, 16)
            load_squares(core, sp, rows_in, "ident", to=dict(ident=core.ident))
            with nc.allow_non_contiguous_dma("gains, one feature per partition; eight logits' weights per row"):
                sp.dma_start(gains["g_pre"], sources["g_pre"].rearrange("(k p) -> p k", p=P)).then_inc(rows_in, 16)
                sp.dma_start(pos_i, a["positions_2"][0].rearrange("(t p) -> p t", p=P)).then_inc(positions_in, 16)
                sp.dma_start(inv, core.inv_freq.broadcast_to([P, ROPE // 2])).then_inc(positions_in, 16)
                sp.dma_start(core.router, a["moe_router_2"][0].rearrange("(k p) e -> p k e", p=P))\
                  .then_inc(core.later_in, 16)
                for key, view in gains.items():
                    if key != "g_pre":
                        sp.dma_start(view, sources[key].rearrange("(k p) -> p k", p=P)).then_inc(core.later_in, 16)
            load_squares(core, sp, core.later_in, "before", "ones", to=dict(before=core.before, ones=core.ones))
            core.later = 16 * (1 + len(gains) - 1 + 2)
            core.load_weights(sp, 0, most=2)
            sp.wait_ge(rows_in, 48)

        @block.gpsimd
        def _(pool):
            pool.memset(table, 1.0).then_inc(last_row, 1)

        @block.tensor
        def _(pe):
            pe.wait_ge(table_wide, 1)
            pe.wait_ge(marking_in, 16)
            for hd in range(AH):
                pe.matmul(ps[hd][:, :], wide_table[0:REL_BUCKETS + 1, hd, :], marking[0:REL_BUCKETS + 1, :],
                          start=True, stop=True).then_inc(rows_ready, 1)

        @block.vector
        def _(dve):
            step = Steps(dve, vector_steps)
            dve.wait_ge(table_in, 16)
            dve.tensor_copy(wide_table[0:REL_BUCKETS + 1, :, :], tall(table[0:REL_BUCKETS + 1, :], P)).then_inc(table_wide, 1)
            for hd in range(AH):
                dve.wait_ge(rows_ready, hd + 1)
                dve.tensor_copy(rows[:, hd, :], ps[hd][:, :]).then_inc(rows_copied, 1)
            dve.wait_ge(positions_in, 32)
            step(dve.tensor_copy(pos, pos_i))
            step(dve.tensor_tensor(angle, tall(pos, ROPE // 2), wide(inv, NT), ALU.mult))
            for out, quarter in ((cos, 0.25), (sin, 0.0)):
                step(dve.tensor_scalar(turns, angle, 1.0 / (2 * math.pi), quarter, ALU.mult, ALU.add))
                step(dve.tensor_scalar(turns, turns, ROUND, None, ALU.add))
                step(dve.tensor_scalar(turns, turns, -ROUND, None, ALU.add))
                step(dve.scalar_tensor_tensor(out=tmp, in0=turns, scalar=-TWO_PI_HI, in1=angle, op0=ALU.mult, op1=ALU.add))
                step(dve.scalar_tensor_tensor(out=tmp, in0=turns, scalar=-TWO_PI_MID, in1=tmp, op0=ALU.mult, op1=ALU.add))
                step(dve.scalar_tensor_tensor(out=tmp, in0=turns, scalar=-TWO_PI_LO, in1=tmp, op0=ALU.mult, op1=ALU.add))
                step(dve.tensor_scalar(tmp, tmp, quarter * 2 * math.pi, None, ALU.add))
                dve.tensor_scalar(out, tmp, PI_SAFE, -PI_SAFE, ALU.min, ALU.max).then_inc(reduced, 1)
                dve.wait_ge(reduced, 1 if quarter else 2)

        @block.scalar
        def _(act):
            act.wait_ge(last_row, 1)
            act.dma_start(table[0:REL_BUCKETS, :], a["rel_bias"]).then_inc(table_in, 16)
            act.dma_start(marking[0:REL_BUCKETS + 1, :], core.buckets).then_inc(marking_in, 16)
            for g in range(2):
                heads = slice(4 * g, 4 * g + 4)
                act.wait_ge(rows_copied, 4 * g + 4)
                act.dma_start(line[heads, 0:P * BANK].rearrange("h (p n) -> p h n", n=BANK), rows[:, heads, :])\
                   .then_inc(core.lines_written, 16)
            for n, out in enumerate((cos, sin)):
                act.wait_ge(reduced, n + 1)
                nc.scalar.activation(out, out, ACT.Sin)
    core.main.back(mark)


def read_bias(core, act, bias):
    line = core.lines
    act.wait_ge(core.lines_written, 32)
    for tt in range(NT):
        first = 255 - P * tt
        askew = line[:, first:first + P * (BANK - 1)].rearrange("h (p n) -> p h n", n=BANK - 1)
        act.dma_start(bias[:, :, tt * SEQ:(tt + 1) * SEQ], askew[:, :, 0:SEQ]).then_inc(core.bias_in, 16)


def rotate(core, q, proj, turned_rows):
    mark = core.main.at
    cos, sin = core.cos, core.sin
    both = core.main.take(NT, 5 * ROPE)
    t = [core.main.take(NT, 5 * 32) for _ in range(4)]
    heads = lambda ap, n: ap.rearrange("p t (h d) -> p t h d", h=n)
    spin = lambda ap: ap.unsqueeze(2).broadcast_to([P, NT, 5, 32])
    with Phase(core, "vector_steps", "pool_steps") as (block, vector_steps, pool_steps):
        @block.sync
        def _(sp):
            core.load_weights(sp, core.consumed)

        @block.vector
        def _(dve):
            step = Steps(dve, vector_steps)
            dve.tensor_copy(heads(both, 5)[:, :, 0:HM, :], heads(q, HM)[:, :, :, NOPE:NOPE + ROPE])
            step(dve.tensor_copy(both[:, :, 4 * ROPE:5 * ROPE], proj[:, :, 640:704]))
            x1, x2 = heads(both, 5)[:, :, :, 0:32], heads(both, 5)[:, :, :, 32:64]
            out = heads(turned_rows, 6)
            dve.tensor_tensor(heads(t[0], 5), x1, spin(cos), ALU.mult)
            dve.tensor_tensor(heads(t[1], 5), x2, spin(sin), ALU.mult)
            dve.tensor_tensor(heads(t[2], 5), x1, spin(sin), ALU.mult)
            step(dve.tensor_tensor(heads(t[3], 5), x2, spin(cos), ALU.mult))
            dve.tensor_tensor(out[:, :, 0:5, 0:32], heads(t[0], 5), heads(t[1], 5), ALU.subtract)
            step(dve.tensor_tensor(out[:, :, 0:5, 32:64], heads(t[2], 5), heads(t[3], 5), ALU.add))
            step(dve.tensor_copy(out[:, :, 5, :], out[:, :, 4, :]))
    core.main.back(mark)


def hgrn(core, proj, mix, layer, a):
    nc, ps = core.nc, core.ps
    main = core.main
    outer = main.at
    hq, hf, hi, hg = (proj[:, :, 704 + 512 * i:704 + 512 * (i + 1)] for i in range(4))
    sq, gain = core.hgrn_squares, core.out_norms[:, layer, :]
    q, k, lf, gate = (main.take(NT, 512) for _ in range(4))
    low = core.bounds
    with Phase(core, "spread_ready", "bound_ready", "sigmoids", "clamped", "logs", "vector_steps") as (
            block, spread_ready, bound_ready, sigmoids, clamped, logs, vector_steps):
        @block.sync
        def _(sp):
            core.load_weights(sp, core.consumed)

        @block.scalar
        def _(act):
            nc.scalar.activation(q, hq, ACT.Sigmoid).then_inc(sigmoids, 1)
            nc.scalar.activation(lf, hf, ACT.Sigmoid).then_inc(sigmoids, 1)
            nc.scalar.activation(k, hf, ACT.Sigmoid, scale=-1.0).then_inc(sigmoids, 1)
            nc.scalar.activation(gate, hg, ACT.Sigmoid).then_inc(sigmoids, 1)
            if layer:
                act.wait_ge(spread_ready, 1)
                nc.scalar.activation(low[:, 0, :], low[:, 0, :], ACT.Sigmoid).then_inc(bound_ready, 1)
            act.wait_ge(clamped, 2)
            nc.scalar.activation(lf, lf, ACT.Ln).then_inc(logs, 1)
            nc.scalar.activation(hf, hf, ACT.Ln).then_inc(logs, 1)

        @block.vector
        def _(dve):
            step = Steps(dve, vector_steps)
            if layer:
                dve.tensor_tensor(low[:, 0, :], low[:, 1, :], low[:, 0, :], ALU.subtract).then_inc(spread_ready, 1)
                dve.wait_ge(bound_ready, 1)
                step(dve.tensor_scalar(low[:, 1, :], low[:, 0, :], -1.0, 1.0, ALU.mult, ALU.add))
                dve.wait_ge(sigmoids, 3)
                step(dve.tensor_tensor(lf, lf, wide(low[:, 1, :], NT), ALU.mult))
                step(dve.tensor_tensor(lf, lf, wide(low[:, 0, :], NT), ALU.add))
                step(dve.tensor_tensor(k, k, wide(low[:, 1, :], NT), ALU.mult))
            dve.wait_ge(sigmoids, 3)
            step(dve.tensor_scalar(lf, lf, 1e-30, None, ALU.max))
            dve.tensor_scalar(hf, lf, 2.0 ** 40, 1.0, ALU.mult, ALU.min).then_inc(clamped, 1)
            dve.wait_ge(clamped, 1)
            dve.tensor_scalar(lf, lf, 2.0 ** -40, None, ALU.max).then_inc(clamped, 1)
            dve.wait_ge(sigmoids, 4)
            step(dve.tensor_tensor(q, q, hq, ALU.mult))
            step(dve.tensor_tensor(gate, gate, hg, ALU.mult))
            dve.wait_ge(logs, 2)
            step(dve.tensor_tensor(lf, lf, hf, ALU.add))

    qT, kT = main.take(4, SEQ), main.take(4, SEQ)
    qT4, kT4 = (t.rearrange("p h (t q) -> p h t q", t=NT) for t in (qT, kT))
    turn(core, [(q, qT, None), (k, kT, None)])

    e = [main.take(NT, 512) for _ in range(2)]
    qk = [q, k]
    att = core.uT[:, 0:4, :].rearrange("p (t a) b -> p t (a b)", t=NT)
    cross = core.uT[:, 4:6, :].rearrange("p a b -> p (a b)")
    o, sqr = q, k
    rms = main.take(3, NT * HH)
    n_levels = LEVELS + 1
    with Phase(core, "sums_ready", "falls_ready", "sides_ready", "scores_ready", "picked", "values_ready",
               "mean_ready", "root_ready", "vector_steps") as (
            block, sums_ready, falls_ready, sides_ready, scores_ready, picked, values_ready, mean_ready,
            root_ready, vector_steps):
        @block.sync
        def _(sp):
            core.load_weights(sp, core.consumed)

        @block.tensor
        def _(pe):
            def sums(n):
                if n >= 2:
                    pe.wait_ge(falls_ready, NT * (n - 1))
                for tt in range(NT):
                    m = sq[f"decay{n}"] if n < LEVELS else sq["after" if tt == 0 else "upto"]
                    for h in range(HH):
                        mm = pe.matmul(ps[2 * (n % 2) + tt][:, h * P:(h + 1) * P], lf[:, tt, h * P:(h + 1) * P], m,
                                       start=True, stop=True)
                mm.then_inc(sums_ready, 1)

            sums(0)
            for h in range(HH):
                for tt in range(NT):
                    mm = pe.matmul(ps[4 + tt][:, h * P:(h + 1) * P], kT4[:, h, tt, :], qT4[:, h, tt, :],
                                   start=True, stop=True)
            mm.then_inc(scores_ready, 1)
            for n in range(n_levels):
                if n + 1 < n_levels:
                    sums(n + 1)
                pe.wait_ge(sides_ready, n + 1)
                side = qk[n % 2]
                if n >= 1:
                    pe.wait_ge(picked, n)
                for tt in range(NT if n < LEVELS else 1):
                    for h in range(HH):
                        cols = slice(h * P, (h + 1) * P)
                        right = side[:, tt, cols] if n < LEVELS else side[:, 1, cols]
                        mm = pe.matmul(ps[4 + 2 * ((n + 1) % 2) + tt][:, cols], side[:, tt, cols], right,
                                       start=True, stop=True)
                mm.then_inc(scores_ready, 1)
            pe.wait_ge(picked, n_levels + 1)
            for tt in range(NT):
                for h in range(HH):
                    cols = slice(h * P, (h + 1) * P)
                    if tt:
                        pe.matmul(ps[tt][:, cols], cross[:, cols], hi[:, 0, cols], start=True, stop=False)
                    mm = pe.matmul(ps[tt][:, cols], att[:, tt, cols], hi[:, tt, cols], start=(tt == 0), stop=True)
            mm.then_inc(values_ready, 1)

        @block.scalar
        def _(act):
            for n in range(n_levels):
                act.wait_ge(sums_ready, n + 1)
                if n >= 2:
                    act.wait_ge(sides_ready, n - 1)
                for tt in range(NT):
                    nc.scalar.activation(e[n % 2][:, tt, :], ps[2 * (n % 2) + tt][:, :], ACT.Exp).then_inc(falls_ready, 1)
            act.wait_ge(mean_ready, 1)
            nc.scalar.activation(rms[:, 1, :], rms[:, 0, :], ACT.Sqrt).then_inc(root_ready, 1)

        @block.vector
        def _(dve):
            step = Steps(dve, vector_steps)

            def pick(n):
                dve.wait_ge(scores_ready, n + 1)
                for tt in range(NT):
                    got = ps[4 + 2 * (n % 2) + tt][:, :].rearrange("p (h t) -> p h t", h=HH)
                    into = att[:, tt, :].rearrange("p (h t) -> p h t", h=HH)
                    if n == 0:
                        last = dve.tensor_tensor(into, got, wide(core.ident, HH), ALU.mult)
                    elif n <= LEVELS:
                        last = dve.copy_predicated(into, wide(sq[f"pick{n - 1}"], HH).bitcast(I32), got)
                    elif tt == 0:
                        last = dve.tensor_copy(cross, ps[4 + 2 * (n % 2)][:, :])
                last.then_inc(picked, 1)

            pick(0)
            for n in range(n_levels):
                dve.wait_ge(falls_ready, NT * (n + 1))
                if n >= 2:
                    dve.wait_ge(scores_ready, n)
                for tt in range(NT):
                    out, fall = qk[n % 2][:, tt, :], e[n % 2][:, tt, :]
                    if n < LEVELS:
                        half = 1 << n
                        blocks = lambda t: t.rearrange("p (b two s) -> p b two s", two=2, s=half)
                        heads = lambda t: t.rearrange("p h (b two s) -> p h b two s", two=2, s=half)
                        o5, f5 = (t.rearrange("p (h b two s) -> p h b two s", h=HH, two=2, s=half) for t in (out, fall))
                        dve.tensor_tensor(o5[:, :, :, 0, :], heads(kT4[:, :, tt, :])[:, :, :, 0, :], f5[:, :, :, 0, :],
                                          ALU.mult)
                        last = dve.tensor_tensor(o5[:, :, :, 1, :], heads(qT4[:, :, tt, :])[:, :, :, 1, :],
                                                 f5[:, :, :, 1, :], ALU.mult)
                    else:
                        src = (kT4 if tt == 0 else qT4)[:, :, tt, :]
                        last = dve.tensor_tensor(out.rearrange("p (h t) -> p h t", h=HH), src,
                                                 fall.rearrange("p (h t) -> p h t", h=HH), ALU.mult)
                last.then_inc(sides_ready, 1)
                pick(n + 1)
            dve.wait_ge(values_ready, 1)
            for tt in range(NT):
                last = dve.tensor_copy(o[:, tt, :], ps[tt][:, :])
            step(last)
            per = lambda t: t.rearrange("p t (h d) -> p (t h) d", d=P)
            step(dve.tensor_tensor(sqr, o, o, ALU.mult))
            step(dve.tensor_reduce(rms[:, 0, :], per(sqr), AX.X, ALU.add))
            dve.tensor_scalar(rms[:, 0, :], rms[:, 0, :], 1.0 / HGV, EPS, ALU.mult, ALU.add).then_inc(mean_ready, 1)
            dve.wait_ge(root_ready, 1)
            step(dve.reciprocal(rms[:, 2, :], rms[:, 1, :]))
            step(dve.tensor_tensor(per(o), per(o), tall(rms[:, 2, :], P), ALU.mult))
            step(dve.tensor_tensor(per(o), per(o), wide(gain, NT * HH), ALU.mult))
            step(dve.tensor_tensor(mix, o, gate, ALU.mult))
    main.back(outer)


HGV = 128


def rms_rows(core, src, gain, into, add, out=None, gain_in=None):
    nc = core.nc
    mark = core.main.at
    normed = core.main.take(NT, DM)
    stat = core.main.take(3, NT)
    with Phase(core, "mean_ready", "root_ready", "rows_ready", "rows_out", "vector_steps") as (
            block, mean_ready, root_ready, rows_ready, rows_out, vector_steps):
        @block.sync
        def _(sp):
            core.load_weights(sp, core.consumed)
            if out is not None:
                for tt in range(NT):
                    sp.wait_ge(rows_ready, tt + 1)
                    sp.dma_start(out[tt * P:(tt + 1) * P, :], into[:, tt, :]).then_inc(rows_out, 16)
                sp.wait_ge(rows_out, 16 * NT)

        @block.scalar
        def _(act):
            act.wait_ge(mean_ready, 1)
            nc.scalar.activation(stat[:, 1, :], stat[:, 1, :], ACT.Sqrt).then_inc(root_ready, 1)

        @block.vector
        def _(dve):
            step = Steps(dve, vector_steps)
            for tt in range(NT):
                last = dve.tensor_tensor_reduce(normed[:, tt, :], src[:, tt, :], src[:, tt, :], 1.0 / DM, 0.0,
                                                ALU.mult, ALU.add, stat[:, 0, tt:tt + 1])
            step(last)
            dve.tensor_scalar(stat[:, 1, :], stat[:, 0, :], EPS, None, ALU.add).then_inc(mean_ready, 1)
            dve.wait_ge(root_ready, 1)
            step(dve.reciprocal(stat[:, 2, :], stat[:, 1, :]))
            if gain_in is not None:
                dve.wait_ge(*gain_in)
            for tt in range(NT):
                dst = normed if add else into
                last = dve.scalar_tensor_tensor(out=dst[:, tt, :], in0=src[:, tt, :], scalar=stat[:, 2, tt:tt + 1],
                                                in1=gain, op0=ALU.mult, op1=ALU.mult)
                if not add:
                    last.then_inc(rows_ready, 1)
            if add:
                step(last)
                step(dve.tensor_tensor(into, into, normed, ALU.add))
    core.main.back(mark)


def route(core, r):
    nc, ps = core.nc, core.ps
    mark = core.main.at
    router, before, ones = core.router, core.before, core.ones
    logits, top, picks = (core.main.take(NT, NE) for _ in range(3))
    index = core.main.take(NT, NE).bitcast(U32)
    names_i = core.main.take(SEQ).bitcast(I32)
    first, second = core.main.take(NT, NE), core.main.take(NT, NE)
    lead = core.main.take(NT)
    share = core.main.take(2, NT)
    count = core.main.take(NE)
    most = core.main.take(2)
    with Phase(core, "numbers_ready", "logits_ready", "lead_ready", "share_ready",
               "chosen_ready", "ranks_ready", "vector_steps") as (
            block, numbers_ready, logits_ready, lead_ready, share_ready, chosen_ready, ranks_ready, vector_steps):
        @block.sync
        def _(sp):
            core.load_weights(sp, core.consumed)

        @block.gpsimd
        def _(pool):
            pool.iota(names_i, [[1, SEQ]], base=0, channel_multiplier=0).then_inc(numbers_ready, 1)

        @block.tensor
        def _(pe):
            for tt in range(NT):
                for k in range(KD):
                    mm = pe.matmul(ps[0][:, tt * NE:(tt + 1) * NE], core.uT[:, k, tt * P:(tt + 1) * P], router[:, k, :],
                                   start=(k == 0), stop=(k == KD - 1))
            mm.then_inc(logits_ready, 1)
            pe.wait_ge(chosen_ready, 1)
            pe.matmul(ps[1][:, 0:NE], before, r.chosen[:, 0, :], start=True, stop=True)
            pe.matmul(ps[1][:, NE:2 * NE], before, r.chosen[:, 1, :], start=True, stop=False)
            pe.matmul(ps[1][:, NE:2 * NE], ones, r.chosen[:, 0, :], start=False, stop=True)
            pe.matmul(ps[1][:, 2 * NE:3 * NE], ones, r.chosen[:, 0, :], start=True, stop=False)
            pe.matmul(ps[1][:, 2 * NE:3 * NE], ones, r.chosen[:, 1, :], start=False, stop=True).then_inc(ranks_ready, 1)

        @block.scalar
        def _(act):
            act.wait_ge(lead_ready, 1)
            nc.scalar.activation(share[:, 0, :], lead, ACT.Sigmoid).then_inc(share_ready, 1)
            nc.scalar.activation(share[:, 1, :], lead, ACT.Sigmoid, scale=-1.0).then_inc(share_ready, 1)

        @block.vector
        def _(dve):
            step = Steps(dve, vector_steps)
            dve.wait_ge(numbers_ready, 1)
            step(dve.tensor_copy(r.numbers, names_i))
            dve.wait_ge(logits_ready, 1)
            step(dve.tensor_copy(logits, ps[0][:, 0:NT * NE].rearrange("p (t e) -> p t e", t=NT)))
            for tt in range(NT):
                step(dve.max(top[:, tt, :], logits[:, tt, :]))
                step(dve.max_index(index[:, tt, :], top[:, tt, :], logits[:, tt, :]))
            step(dve.tensor_copy(picks, index))
            dve.tensor_tensor(lead, top[:, :, 0], top[:, :, 1], ALU.subtract).then_inc(lead_ready, 1)
            for tt in range(NT):
                for n, out in enumerate((first, second)):
                    step(dve.tensor_scalar(out[:, tt, :], r.numbers[:, 0:NE], picks[:, tt, n:n + 1], None, ALU.is_equal))
            dve.tensor_tensor(r.chosen, first, second, ALU.add).then_inc(chosen_ready, 1)
            dve.wait_ge(chosen_ready, 1)
            dve.wait_ge(share_ready, 2)
            for tt in range(NT):
                step(dve.tensor_scalar(first[:, tt, :], first[:, tt, :], share[:, 0, tt:tt + 1], None, ALU.mult))
                step(dve.scalar_tensor_tensor(out=r.gate[:, tt, :], in0=second[:, tt, :], scalar=share[:, 1, tt:tt + 1],
                                              in1=first[:, tt, :], op0=ALU.mult, op1=ALU.add))
            dve.wait_ge(ranks_ready, 1)
            step(dve.tensor_copy(r.rank, ps[1][:, 0:NT * NE].rearrange("p (t e) -> p t e", t=NT)))
            step(dve.tensor_copy(count, ps[1][:, 2 * NE:3 * NE]))
            step(dve.tensor_reduce(most[:, 0:1], count, AX.X, ALU.max))
            step(dve.tensor_scalar(most[:, 1:2], most[:, 0:1], P + 0.5, None, ALU.is_gt))
            step(dve.tensor_copy(r.flag, most[:, 1:2]))
    core.main.back(mark)


class Routing:

    def __init__(self, core):
        take = core.main.take
        self.chosen, self.gate, self.rank = take(NT, NE), take(NT, NE), take(NT, NE)
        self.numbers = take(SEQ)
        self.flag = take(1).bitcast(I32)
        self.place = take(NT, (NE + 1) * P)
        self.spreadT = take(NE * SEQ)


def when(eng, flag):
    stack = ExitStack()
    if flag is not None:
        stack.enter_context(eng.If(eng.value_load(flag[0:1, 0:1], min_val=0, max_val=1) > 0))
    return stack


def experts(core, a, r, xn, gain, base, flag):
    nc, ps, h = core.nc, core.ps, core.h
    mark = core.main.at
    gated = core.main.take(NT, NE * P)
    with Phase(core, "vector_steps", "places_ready", "turned", "copied") as (
            block, vector_steps, places_ready, turned, copied):
        @block.sync
        def _(sp):
            if flag is None:
                core.load_weights(sp, core.consumed)

        @block.vector
        def _(dve):
            with when(dve, flag):
                slots = r.numbers[:, base:base + P]
                for e in range(NE + 1):
                    for tt in range(NT):
                        cols = slice(e * P, (e + 1) * P)
                        if e == NE:
                            dve.memset(r.place[:, tt, cols], 0.0)
                            continue
                        dve.tensor_scalar(r.place[:, tt, cols], slots, r.rank[:, tt, e:e + 1],
                                          r.chosen[:, tt, e:e + 1], ALU.is_equal, ALU.mult)
                        last = dve.tensor_scalar(gated[:, tt, cols], slots, r.rank[:, tt, e:e + 1],
                                                 r.gate[:, tt, e:e + 1], ALU.is_equal, ALU.mult)
                    if e < NE:
                        last.then_inc(places_ready, 1)
                for n in range(4):
                    dve.wait_ge(turned, n + 1)
                    dve.tensor_copy(r.spreadT[:, n * BANK:(n + 1) * BANK], ps[n][:, :]).then_inc(copied, 1)
                dve.wait_ge(copied, 4)

        @block.tensor
        def _(pe):
            with when(pe, flag):
                for e in range(NE):
                    pe.wait_ge(places_ready, e + 1)
                    for tt in range(NT):
                        c = (2 * e + tt) % 4
                        mm = pe.transpose(ps[e // 2][:, c * P:(c + 1) * P], gated[:, tt, e * P:(e + 1) * P], core.ident)
                    if e % 2:
                        mm.then_inc(turned, 1)
    core.main.back(mark)

    NC = EF // BANK
    LOADS = 3 * NC
    xgT = core.main.take(KD, P)
    hid = core.main.take(EF)
    hidT = core.main.take(EF // P, P)
    silu = core.main.take(2, BANK)
    ys = core.main.take(DM)
    spread_now = core.main.take(SEQ)
    w_gate, w_up, w_down = (a[n][0] for n in ("moe_w_gate_2", "moe_w_up_2", "moe_w_down_2"))
    used0, landed0 = core.moe_used, list(core.moe_landed)

    def weight(e, i):
        if i < 2 * NC:
            w = (w_gate, w_up)[i % 2]
            c = i // 2
            return w[e, :, c * BANK:(c + 1) * BANK].rearrange("(k p) n -> p k n", p=P)
        c = i - 2 * NC
        return w_down[e, c * BANK:(c + 1) * BANK, :].rearrange("(k p) n -> p k n", p=P)

    def slot(i):
        if i < 2 * NC:
            return core.ring[:, i % SLOTS, :].rearrange("p (k n) -> p k n", n=BANK)
        return core.ring[:, i % SLOTS, :].rearrange("p (k n) -> p k n", n=DM)

    with Phase(core, "gathered", "gathered_copied", "gate_ready", "up_ready", "silu_ready", "hid_ready", "turned",
               "hidT_ready", "down_ready", "ys_by_vector", "ys_by_scalar", "spread_ready", "scattered", "added", "slots_granted") as (
            block, gathered, gathered_copied, gate_ready, up_ready, silu_ready, hid_ready, turned, hidT_ready,
            down_ready, ys_by_vector, ys_by_scalar, spread_ready, scattered, added, slots_granted):
        @block.sync
        def _(sp):
            def load(e, i):
                if isinstance(e, int) and LOADS * e + i < SLOTS:
                    if flag is not None:
                        sp.wait_ge(core.weights_used, used0 + LOADS * e + i - SLOTS + 1)
                else:
                    sp.wait_ge(core.weights_used, e * LOADS + (used0 + i - SLOTS + 1))
                    sp.sem_inc(slots_granted, 1)
                sp.dma_start(slot(i), weight(e, i)).then_inc(core.landed[i % SLOTS], 16)

            with when(sp, flag):
                if flag is not None:
                    for i in range(SLOTS):
                        load(0, i)
                with sp.Fori(0, NE - 1) as e:
                    for i in range(SLOTS, LOADS):
                        load(e, i)
                    for i in range(SLOTS):
                        load(e + 1, i)
                for i in range(SLOTS, LOADS):
                    load(NE - 1, i)

        @block.tensor
        def _(pe):
            with when(pe, flag):
                def gather(e, release=None):
                    for k in range(KD):
                        for tt in range(NT):
                            mm = pe.matmul(ps[4 + k // 4][:, (k % 4) * P:(k % 4 + 1) * P], xn[:, tt, k * P:(k + 1) * P],
                                           r.place.rearrange("p t (e s) -> p t e s", s=P)[:, tt, e, :], start=(tt == 0), stop=(tt == NT - 1))
                            if release is not None and k + tt == 0:
                                mm.then_inc(core.weights_used, 1)
                        if k % 4 == 3:
                            mm.then_inc(gathered, 1)

                def turn_chunk(e, c):
                    pe.wait_ge(hid_ready, e * NC + (c + 3))
                    if c >= 2:
                        pe.wait_ge(hidT_ready, e * NC + (c - 1))
                    for k in range(4):
                        mm = pe.transpose(ps[4 + c % 2][:, k * P:(k + 1) * P], hid[:, (4 * c + k) * P:(4 * c + k + 1) * P],
                                          core.ident)
                    mm.then_inc(turned, 1)

                gather(0)
                with pe.Fori(0, NE) as e:
                    pe.wait_ge(gathered_copied, e * 2 + 2)
                    for i in range(2 * NC):
                        c = i // 2
                        if i % 2 == 0:
                            pe.wait_ge(hid_ready, e * NC + (2 if c == 0 else c + 1))
                            if c < 2:
                                pe.wait_ge(added, e * 4 + (2 + 2 * c))
                        pe.wait_ge(core.landed[i % SLOTS], e * 48 + (landed0[i % SLOTS] + 16 * (i // SLOTS)))
                        for k in range(KD):
                            mm = pe.matmul(ps[2 * (c % 2) + i % 2][:, :], xgT[:, k, :], slot(i)[:, k, :], start=(k == 0),
                                           stop=(k == KD - 1))
                            if k == 0 and i:
                                mm.then_inc(core.weights_used, 1)
                        mm.then_inc(up_ready if i % 2 else gate_ready, 1)
                        if i % 2 and c:
                            turn_chunk(e, c - 1)
                    turn_chunk(e, NC - 1)
                    for c in range(NC):
                        i = 2 * NC + c
                        pe.wait_ge(hidT_ready, e * NC + (c + 1))
                        pe.wait_ge(core.landed[i % SLOTS], e * 48 + (landed0[i % SLOTS] + 16 * (i // SLOTS)))
                        for half in range(2):
                            for k in range(4):
                                mm = pe.matmul(ps[6 + half][:, :], hidT[:, 4 * c + k, :],
                                               slot(i)[:, k, half * BANK:(half + 1) * BANK],
                                               start=(c + k == 0), stop=(c == NC - 1 and k == 3))
                                if half + k == 0:
                                    mm.then_inc(core.weights_used, 1)
                    mm.then_inc(down_ready, 1)
                    gather(e + 1, release=True)
                    pe.wait_ge(ys_by_vector, e + 1)
                    pe.wait_ge(ys_by_scalar, e + 1)
                    pe.wait_ge(spread_ready, e + 1)
                    for tt in range(NT):
                        for half in range(2):
                            pe.matmul(ps[2 * tt + half][:, :], spread_now[:, tt * P:(tt + 1) * P],
                                      ys[:, half * BANK:(half + 1) * BANK], start=True, stop=True).then_inc(scattered, 1)

        @block.scalar
        def _(act):
            with when(act, flag):
                with act.Fori(0, NE) as e:
                    def copy_turned(c):
                        act.wait_ge(turned, e * NC + (c + 1))
                        nc.scalar.copy(hidT[:, 4 * c:4 * c + 4, :], ps[4 + c % 2][:, :].rearrange("p (k t) -> p k t", t=P))\
                          .then_inc(hidT_ready, 1)

                    for c in range(NC):
                        act.wait_ge(gate_ready, e * NC + (c + 1))
                        act.wait_ge(hid_ready, e * NC + (2 if c == 0 else c + 1))
                        nc.scalar.activation(silu[:, c % 2, :], ps[2 * (c % 2)][:, :], ACT.Silu).then_inc(silu_ready, 1)
                        if c:
                            copy_turned(c - 1)
                    copy_turned(NC - 1)
                    act.wait_ge(down_ready, e + 1)
                    nc.scalar.copy(ys[:, BANK:DM], ps[7][:, :]).then_inc(ys_by_scalar, 1)

        @block.vector
        def _(dve):
            with when(dve, flag):
                def take_gathered(e2):
                    for g in range(2):
                        dve.wait_ge(gathered, e2 + (g + 1))
                        dve.tensor_tensor(xgT[:, 4 * g:4 * g + 4, :], ps[4 + g][:, :].rearrange("p (k t) -> p k t", t=P),
                                          tall(gain[:, 4 * g:4 * g + 4], P), ALU.mult).then_inc(gathered_copied, 1)

                dve.nop().then_inc(hid_ready, 2)
                dve.nop().then_inc(added, 4)
                take_gathered(0)
                with dve.Fori(0, NE) as e:
                    dve.tensor_copy(spread_now, r.spreadT.rearrange("p (e t) -> p e t", t=SEQ)[:, e, :]).then_inc(spread_ready, 1)
                    for c in range(NC):
                        dve.wait_ge(silu_ready, e * NC + (c + 1))
                        dve.wait_ge(up_ready, e * NC + (c + 1))
                        dve.tensor_tensor(hid[:, c * BANK:(c + 1) * BANK], silu[:, c % 2, :], ps[2 * (c % 2) + 1][:, :],
                                          ALU.mult).then_inc(hid_ready, 1)
                    dve.wait_ge(down_ready, e + 1)
                    dve.tensor_copy(ys[:, 0:BANK], ps[6][:, :]).then_inc(ys_by_vector, 1)
                    take_gathered(e * 2 + 2)
                    for tt in range(NT):
                        for half in range(2):
                            dve.wait_ge(scattered, e * 4 + (2 * tt + half + 1))
                            cols = slice(half * BANK, (half + 1) * BANK)
                            dve.tensor_tensor(h[:, tt, cols], h[:, tt, cols], ps[2 * tt + half][:, :], ALU.add)\
                               .then_inc(added, 1)
    core.main.back(mark)
    core.moe_used += LOADS * NE
    core.moe_landed = [n + 48 * NE for n in core.moe_landed]


def program(nc, a, out, constants):
    ctx = ExitStack()
    with ctx:
        core = Core(nc, ctx)
        core.squares, core.buckets, causal_dram, core.inv_freq, core.chunk_pairs = constants
        main = core.main
        core.scratch = Region(core.ring[:, 5:7, :].rearrange("p a n -> p (a n)"), 2 * SLOT)
        core.h = h = main.take(NT, DM)
        core.uT = uT = main.take(KD, SEQ)
        core.ident = main.take(P)
        gains = dict(g_pre=main.take(KD))
        sources = dict(g_pre=a["g_pre"][0])
        for layer in range(2):
            for n, d in (("mix_norm_2", DM), ("ffn_norm_2", DM), ("q_a_norm_2", QR), ("kv_a_norm_2", KVR)):
                gains[n, layer] = main.take(d // P)
                sources[n, layer] = a[n][layer]
        core.cos, core.sin = main.take(NT, ROPE // 2), main.take(NT, ROPE // 2)

        def columns(w, c0, width, slots=SLOTS):
            return core.add_weights(w[:, c0:c0 + width].rearrange("(k p) n -> p k n", p=P), w.shape[0] // P, width, slots)

        def rows(w, k0, tiles, slots=SLOTS):
            return core.add_weights(w[k0 * P:(k0 + tiles) * P, :].rearrange("(k p) n -> p k n", p=P), tiles, w.shape[1], slots)

        w_in = a["w_in"][0]
        in_cols = [(c, BANK) for c in range(0, 4 * AW, BANK)] + \
                  [(4 * AW + c, min(BANK, RW - c)) for c in range(0, RW, BANK)] + \
                  [(4 * AW + RW + c, BANK) for c in range(0, 2 * DM, BANK)]
        c_in = [columns(w_in, c, w, 5) for c, w in in_cols]
        c_pa, c_pb = rows(a["p_a"][0], 0, 4, 5), rows(a["p_b"][0], 0, 4, 5)
        c_out = [columns(a["w_out"][0], c, BANK, 5) for c in (0, BANK)]
        c_up = rows(a["w_ple_up"][0], 0, 2, 5)
        c_ple = [columns(a["w_ple_gate"][0], c, BANK) for c in (0, BANK)]
        in2_cols = [(c, min(BANK, IN2 - c)) for c in range(0, IN2, BANK)]
        ff_cols = [(c, min(BANK, FF - c)) for c in range(0, FF, BANK)]
        layers = []
        for layer in range(2):
            p = dict(in2=[columns(a["w_in_2"][layer], c, w) for c, w in in2_cols],
                     qb=columns(a["w_q_b_2"][layer], 0, 768), kvb=columns(a["w_kv_b_2"][layer], 0, 1024),
                     out2=[columns(a["w_out_2"][layer], c, BANK) for c in (0, BANK)])
            if layer == 0:
                p["gate"] = [columns(a["dense_w_gate_2"][0], c, w) for c, w in ff_cols]
                p["up"] = [columns(a["dense_w_up_2"][0], c, w) for c, w in ff_cols]
                p["down"] = [(k, min(4, FF // P - k)) for k in range(0, FF // P, 4)]
                p["down"] = [(rows(a["dense_w_down_2"][0], k, n), k, n) for k, n in p["down"]]
            layers.append(p)
        core.moe_used = len(core.plan)
        for i in range(SLOTS):
            w = a[("moe_w_gate_2", "moe_w_up_2")[i % 2]][0, 0]
            c = i // 2
            core.add_weights(w[:, c * BANK:(c + 1) * BANK].rearrange("(k p) n -> p k n", p=P), KD, BANK, slot=i)
        core.moe_landed = [core.plan[core.moe_used + i]["landed"] for i in range(SLOTS)]

        core.slots_now = 5
        core.lines_written = ctx.enter_context(nc.semaphore("lines_written"))
        core.bias_in = ctx.enter_context(nc.semaphore("bias_in"))
        core.later_in = ctx.enter_context(nc.semaphore("later_in"))
        core.router, core.before, core.ones = main.take(KD, NE), main.take(P), main.take(P)
        bias = core.scratch.take(AH, BANK)
        bias_rows = core.scratch.take(AH, BANK)
        begin(core, a, bias, bias_rows, gains, sources)

        turn(core, [(h, uT, gains["g_pre"])], rms=True)
        ya, yb = main.take(NT, AW), main.take(NT, BW)
        gates = main.take(NT, 2 * DM)
        rw = main.take(NT, RW)
        block_one = main.at
        acol = main.take(NT, 4 * AW)

        def store_in(eng, steps, item, psum):
            g, _, tt = item
            c, w = in_cols[g]
            if c < 4 * AW:
                dst = acol[:, tt, c:c + w]
                if c >= 3 * AW:
                    return eng.activation(dst, psum[:, 0:w], ACT.Silu)
            elif c < 4 * AW + RW:
                dst = rw[:, tt, c - 4 * AW:c - 4 * AW + w]
            else:
                c -= 4 * AW + RW
                return eng.activation(gates[:, tt, c:c + w], psum[:, 0:w], ACT.Sigmoid)
            return eng.tensor_copy(dst, psum[:, 0:w])

        def reads_in(item):
            c = in_cols[item[0]][0]
            return "scalar" if c == 3 * AW or c >= 4 * AW + RW else "vector"

        gemm(core, uT, [([(ch, 0, KD)], [(0, w)]) for ch, (_, w) in zip(c_in, in_cols)], store_in, reads_in,
             beside=lambda act: read_bias(core, act, bias))

        qkT = uT
        turn(core, [(acol[:, :, 0:AW], qkT[:, 0:4, :], None), (acol[:, :, AW:2 * AW], qkT[:, 4:8, :], None)])

        def scores_a(hd, tt):
            rows_of = slice(64 * (hd % 2), 64 * (hd % 2) + 64)
            return [(qkT[rows_of, hd // 2, tt * P:(tt + 1) * P], qkT[rows_of, 4 + hd // 2, :])]

        zs = acol[:, :, 3 * AW:4 * AW]

        def finish_a(dve, hd, tt, product, recip):
            cols = slice(hd * AD, (hd + 1) * AD)
            return dve.scalar_tensor_tensor(out=ya[:, tt, cols], in0=product, scalar=recip, in1=zs[:, tt, cols],
                                            op0=ALU.mult, op1=ALU.mult)

        attention(core, AH, scores_a, AD ** -0.5, lambda hd: bias[:, hd, :],
                  lambda hd, kt: acol[:, kt, 2 * AW + hd * AD:2 * AW + (hd + 1) * AD], finish_a, AD,
                  (core.bias_in, 32))
        main.back(block_one)
        core.scratch.back(0)
        rwkv(core, rw, yb, a)
        core.slots_now = SLOTS
        main.back(block_one)
        hgrn_names = [f"decay{n}" for n in range(LEVELS)] + [f"pick{n}" for n in range(LEVELS)] + ["after", "upto"]
        whole_main = main.size
        hgrn_sq = main.take_top(len(hgrn_names), P)
        core.hgrn_squares = {n: hgrn_sq[:, i, :] for i, n in enumerate(hgrn_names)}
        core.out_norms = main.take_top(2, P)
        core.bounds = main.take_top(2, 512)
        causal = main.take_top(NT * SEQ)
        g_post = main.take(DM)
        p_rows = rw[:, 0, 0:NT * PLE].rearrange("p (t d) -> p t d", t=NT)
        with Phase(core) as (block,):
            @block.sync
            def _(sp):
                sp.dma_start(g_post, spread(a["g_post"][0], P)).then_inc(core.later_in, 16)
                sp.dma_start(p_rows, a["p"][0, 0].rearrange("(t p) d -> p t d", p=P)).then_inc(core.later_in, 16)
                sp.dma_start(causal, causal_dram).then_inc(core.later_in, 16)
                load_squares(core, sp, core.later_in, *hgrn_names, to=core.hgrn_squares)
                for i in range(2):
                    sp.dma_start(core.out_norms[:, i, :], spread(a["hg_out_norm_2"][i], P)).then_inc(core.later_in, 16)
                    sp.dma_start(core.bounds[:, i, :], spread(a["hg_lower_bounds_2"][i], P)).then_inc(core.later_in, 16)
                core.load_weights(sp, core.consumed)
        core.later += 16 * (3 + len(hgrn_names) + 4)

        turn(core, [(ya, uT[:, 0:4, :], None), (yb, uT[:, 4:8, :], None)])

        def merge(eng, steps, item, psum):
            g, c, tt = item
            view = gates[:, tt, g * DM + c * BANK:g * DM + (c + 1) * BANK]
            if g == 0:
                return eng.tensor_tensor(view, view, psum[:, :], ALU.mult)
            steps(eng.tensor_tensor(view, view, psum[:, :], ALU.mult))
            first = gates[:, tt, c * BANK:(c + 1) * BANK]
            return eng.tensor_tensor(first, first, view, ALU.add)

        always_vector = lambda item: "vector"
        halves = [(0, BANK), (BANK, BANK)]
        gemm(core, uT, [([(c_pa, 0, 4)], halves), ([(c_pb, 4, 4)], halves)], merge, always_vector)
        merged = gates[:, :, 0:DM]
        turn(core, [(merged, uT, None)])
        y = gates[:, :, DM:2 * DM]

        def store(dst):
            def evacuate(eng, steps, item, psum):
                g, _, tt = item
                out_ = dst[:, tt, g * BANK:g * BANK + min(BANK, dst.shape[2] - g * BANK)]
                got = psum[:, 0:out_.shape[1]]
                return eng.copy(out_, got) if eng is nc.scalar else eng.tensor_copy(out_, got)
            return evacuate

        alternate = lambda item: "scalar" if item[2] else "vector"
        gemm(core, uT, [([(ch, 0, KD)], [(0, BANK)]) for ch in c_out], store(y), alternate)
        with Phase(core) as (block,):
            @block.sync
            def _(sp):
                core.load_weights(sp, core.consumed)
                sp.wait_ge(core.later_in, core.later)
        rms_rows(core, y, g_post, h, True)

        pT = rw[:, 1, 0:NT * PLE].rearrange("p (t d) -> p t d", t=NT)
        turn(core, [(p_rows, pT, None), (h, uT, None)])
        embed = gates[:, :, 0:DM]

        def store_embed(eng, steps, item, psum):
            _, c, tt = item
            return eng.tensor_copy(embed[:, tt, c * BANK:(c + 1) * BANK], psum[:, :])

        gemm(core, pT, [([(c_up, 0, 2)], halves)], store_embed, always_vector)
        sig = gates[:, :, DM:2 * DM]
        gemm(core, uT, [([(ch, 0, KD)], [(0, BANK)]) for ch in c_ple],
             lambda eng, steps, item, psum: eng.activation(sig[:, item[2], item[0] * BANK:(item[0] + 1) * BANK],
                                                           psum[:, :], ACT.Sigmoid), lambda item: "scalar")
        with Phase(core, "vector_steps") as (block, vector_steps):
            @block.sync
            def _(sp):
                core.load_weights(sp, core.consumed)

            @block.vector
            def _(dve):
                step = Steps(dve, vector_steps)
                step(dve.tensor_tensor(sig, sig, embed, ALU.mult))
                step(dve.tensor_tensor(h, h, sig, ALU.add))
        main.back(block_one - NT * RW - NT * 2 * DM - 2 * NT * AW)

        def add_to_h(eng, steps, item, psum):
            g, c, tt = item
            cols = slice((g + c) * BANK, (g + c + 1) * BANK)
            return eng.tensor_tensor(h[:, tt, cols], h[:, tt, cols], psum[:, :], ALU.add)

        for layer, plan in enumerate(layers):
            start = main.at
            turn(core, [(h, uT, gains["mix_norm_2", layer])], rms=True)
            mix = main.take(NT, DM)
            proj = main.take(NT, IN2)
            gemm(core, uT, [([(ch, 0, KD)], [(0, w)]) for ch, (_, w) in zip(plan["in2"], in2_cols)], store(proj),
                 alternate)
            latent = main.at
            q, kv = main.take(NT, 768), main.take(NT, 1024)
            cqT, ckvT = uT[:, 0:3, :], uT[:, 3:5, :]
            turn(core, [(proj[:, :, 0:QR], cqT, gains["q_a_norm_2", layer]),
                        (proj[:, :, QR:QR + KVR], ckvT, gains["kv_a_norm_2", layer])], rms=True)

            def store_parts(dst, widths):
                def evacuate(eng, steps, item, psum):
                    _, c, tt = item
                    c0, w = widths[c]
                    out_ = dst[:, tt, c0:c0 + w]
                    return eng.copy(out_, psum[:, 0:w]) if eng is nc.scalar else eng.tensor_copy(out_, psum[:, 0:w])
                return evacuate

            q_parts = [(0, BANK), (BANK, 256)]
            gemm(core, cqT, [([(plan["qb"], 0, QR // P)], q_parts)], store_parts(q, q_parts), alternate)
            gemm(core, ckvT, [([(plan["kvb"], 0, KVR // P)], halves)], store_parts(kv, halves), alternate)
            spun = main.take(NT, 6 * ROPE)
            rotate(core, q, proj, spun)
            spunT = main.take(3, SEQ)
            heads_at = main.at
            nopes = main.take(NT, 2 * HM * NOPE)
            with Phase(core) as (block,):
                @block.vector
                def _(dve):
                    for n, (src, d) in enumerate(((q, NOPE + ROPE), (kv, NOPE + VD))):
                        dve.tensor_copy(nopes[:, :, n * 512:(n + 1) * 512].rearrange("p t (h d) -> p t h d", h=HM),
                                        src.rearrange("p t (h d) -> p t h d", d=d)[:, :, :, 0:NOPE])
            turn(core, [(nopes, uT, None), (spun, spunT, None)])
            main.back(heads_at)
            kpe = main.take(2, SEQ)
            with Phase(core, "zeroed") as (block, zeroed):
                @block.vector
                def _(dve):
                    dve.memset(kpe, 0.0).then_inc(zeroed, 1)
                    dve.wait_ge(zeroed, 1)
                    for par in range(2):
                        half = slice(64 * par, 64 * par + 64)
                        dve.tensor_copy(kpe[half, par, :], spunT[half, 2, :])

            def scores_m(hd, tt):
                rows_of = slice(tt * P, (tt + 1) * P)
                return [(uT[:, hd, rows_of], uT[:, HM + hd, :]), (spunT[:, hd // 2, rows_of], kpe[:, hd % 2, :])]

            def finish_m(dve, hd, tt, product, recip):
                return dve.tensor_scalar(mix[:, tt, hd * VD:(hd + 1) * VD], product, recip, None, ALU.mult)

            attention(core, HM, scores_m, (NOPE + ROPE) ** -0.5, lambda hd: causal,
                      lambda hd, kt: kv[:, kt, hd * 256 + NOPE:(hd + 1) * 256], finish_m, VD)
            main.back(latent)
            hgrn(core, proj, mix[:, :, 512:1024], layer, a)
            turn(core, [(mix, uT, None)])
            gemm(core, uT, [([(ch, 0, KD)], [(0, BANK)]) for ch in plan["out2"]], add_to_h, always_vector)
            main.back(start)
            if layer == 0:
                turn(core, [(h, uT, gains["ffn_norm_2", layer])], rms=True)
                hid = main.take(NT, FF)
                gemm(core, uT, [([(ch, 0, KD)], [(0, w)]) for ch, (_, w) in zip(plan["gate"], ff_cols)],
                     lambda eng, steps, item, psum: eng.activation(
                         hid[:, item[2], ff_cols[item[0]][0]:sum(ff_cols[item[0]])], psum[:, 0:ff_cols[item[0]][1]],
                         ACT.Silu), lambda item: "scalar")

                def times_up(eng, steps, item, psum):
                    c, w = ff_cols[item[0]]
                    view = hid[:, item[2], c:c + w]
                    return eng.tensor_tensor(view, view, psum[:, 0:w], ALU.mult)

                gemm(core, uT, [([(ch, 0, KD)], [(0, w)]) for ch, (_, w) in zip(plan["up"], ff_cols)], times_up,
                     always_vector)
                hidT = main.take(FF // P, SEQ)
                turn(core, [(hid, hidT, None)])
                gemm(core, hidT, [(plan["down"], halves)], add_to_h, always_vector)
            else:
                main.size = whole_main
                final_gain = main.take(DM)
                kept = main.at
                final_in = ctx.enter_context(nc.semaphore("final_in"))
                with Phase(core) as (block,):
                    @block.sync
                    def _(sp):
                        sp.dma_start(final_gain, spread(a["final_norm_2"], P)).then_inc(final_in, 16)
                xn = main.take(NT, DM)
                turn(core, [(h, uT, gains["ffn_norm_2", layer])], rms=True, keep=[xn])
                r = Routing(core)
                route(core, r)
                experts(core, a, r, xn, gains["ffn_norm_2", layer], 0, None)
                experts(core, a, r, xn, gains["ffn_norm_2", layer], P, r.flag)
                start = kept
            main.back(start)
        rms_rows(core, h, final_gain, uT.rearrange("p k (a n) -> p (k a) n", a=1)
                 .rearrange("p (t k) n -> p t (k n)", t=NT), False, out[0],
                 (final_in, 16))


_INS = ["x", "p", "g_pre", "w_in", "rel_bias", "mu_shift", "w0", "w_up", "a0", "a_up", "k_k", "k_a", "r_k",
        "ln_x_w", "ln_x_b", "p_a", "p_b", "w_out", "g_post", "w_ple_up", "w_ple_gate", "positions_2",
        "mix_norm_2", "w_in_2", "q_a_norm_2", "w_q_b_2", "kv_a_norm_2", "w_kv_b_2", "hg_lower_bounds_2",
        "hg_out_norm_2", "w_out_2", "ffn_norm_2", "dense_w_gate_2", "dense_w_up_2", "dense_w_down_2",
        "moe_router_2", "moe_w_gate_2", "moe_w_up_2", "moe_w_down_2", "final_norm_2"]


def kernel(**inputs):
    import numpy as _np
    import concourse.bacc as _bacc
    from concourse import mybir as _mybir
    from concourse.bass_utils import run_bass_kernel_spmd as _run

    nc = _bacc.Bacc("TRN2", target_bir_lowering=False, num_devices=1)
    arrays, args = {}, {}
    for name in _INS:
        x = _np.ascontiguousarray(inputs[name])
        arrays[f"in_{name}"] = x
        args[name] = nc.dram_tensor(f"in_{name}", x.shape, _mybir.dt.from_np(x.dtype), kind="ExternalInput").ap()
    constants = []
    for name, c in (("squares", square_constants()), ("buckets", bucket_constants()), ("causal", causal_constants()),
                    ("inv_freq", rope_constants()), ("chunk_pairs", chunk_constants())):
        c = _np.ascontiguousarray(c, dtype=_np.float32)
        arrays[f"const_{name}"] = c
        constants.append(nc.dram_tensor(f"const_{name}", c.shape, F32, kind="ExternalInput").ap())
    out = nc.dram_tensor("out", (1, SEQ, DM), F32, kind="ExternalOutput").ap()
    program(nc, args, out, constants)
    r = _run(nc, [arrays], core_ids=[0])
    return r.results[0]["out"]
```
